# Optimizing a Trainium2 kernel written in Bass

```python
import math
import jax, jax.numpy as jnp
from jax import lax
import numpy as np

D_MODEL = 1024
BATCH = 1
SEQ = 256
DEPTH = 2

ATTN_HEADS = 8
HEAD_DIM = 64
ATTN_WIDTH = ATTN_HEADS * HEAD_DIM
CONV_GROUPS = 8
CONV_WIDTH = D_MODEL - ATTN_WIDTH
CONV_KERNEL = 31
MIX_IN = 3 * ATTN_WIDTH + 2 * CONV_WIDTH
ROPE_THETA = 10000.0
MOBA_BLOCK = 256
MOBA_TOPK = 3
MOBA_Q_CHUNK = 32
PEER_HEADS = 8
PEER_NKEYS = 128
PEER_EXPERTS = PEER_NKEYS * PEER_NKEYS
PEER_QDIM = 256
PEER_HALF = PEER_QDIM // 2
PEER_TOPK = 16
PEER_TOK_CHUNK = 128
DEEPNORM_ALPHA = (2 * DEPTH) ** 0.25
DEEPNORM_BETA = (8 * DEPTH) ** -0.25
LN_EPS = 1e-5

kernel_name = "hymba_moba_conformer_peer_deepnorm"

def layer_norm(x, g, b):
    xf = x.astype(jnp.float32)
    mu = jnp.mean(xf, axis=-1, keepdims=True)
    xc = xf - mu
    var = jnp.mean(xc * xc, axis=-1, keepdims=True)
    y = xc * lax.rsqrt(var + LN_EPS) * g.astype(jnp.float32) + b.astype(jnp.float32)
    return y.astype(x.dtype)

def rope_tables(S):
    pos = jnp.arange(S, dtype=jnp.float32)
    inv = jnp.power(ROPE_THETA, -jnp.arange(0, HEAD_DIM, 2, dtype=jnp.float32) / HEAD_DIM)
    ang = pos[:, None] * inv[None, :]
    return jnp.cos(ang), jnp.sin(ang)

def apply_rope(t, cos, sin):
    tf = t.astype(jnp.float32)
    half = HEAD_DIM // 2
    t1, t2 = tf[..., :half], tf[..., half:]
    out = jnp.concatenate([t1 * cos - t2 * sin, t2 * cos + t1 * sin], axis=-1)
    return out.astype(t.dtype)

def split_heads(t, B, S):
    return t.reshape(B, S, ATTN_HEADS, HEAD_DIM).transpose(0, 2, 1, 3)

def moba_attention(q, k, v):
    B, H, S, Dh = q.shape
    nb = -(-S // MOBA_BLOCK)
    sp = nb * MOBA_BLOCK
    pad = ((0, 0), (0, 0), (0, sp - S), (0, 0))
    kb = jnp.pad(k, pad).reshape(B, H, nb, MOBA_BLOCK, Dh)
    vb = jnp.pad(v, pad).reshape(B, H, nb, MOBA_BLOCK, Dh)
    k_mean = jnp.mean(kb.astype(jnp.float32), axis=3)
    gate = jnp.einsum('bhsd,bhnd->bhsn', q.astype(jnp.float32), k_mean)
    q_blk = jnp.arange(S) // MOBA_BLOCK
    fully_past = jnp.arange(nb)[None, :] < q_blk[:, None]
    gate = jnp.where(fully_past, gate, -jnp.inf)
    n_sel = max(1, min(MOBA_TOPK, nb - 1))
    sel_score, sel_idx = lax.top_k(gate, n_sel)
    sel_valid = jnp.isfinite(sel_score)

    nc = S // MOBA_Q_CHUNK
    scale = HEAD_DIM ** -0.5
    b_ix = jnp.arange(B)[:, None, None, None]
    h_ix = jnp.arange(H)[None, :, None, None]

    def to_chunks(a):
        a = a.reshape(B, H, nc, MOBA_Q_CHUNK, *a.shape[3:])
        return jnp.moveaxis(a, 2, 0)

    def chunk_fn(args):
        q_c, idx_c, valid_c, start = args
        k_sel = kb[b_ix, h_ix, idx_c]
        v_sel = vb[b_ix, h_ix, idx_c]
        own = start // MOBA_BLOCK
        k_own = lax.dynamic_index_in_dim(kb, own, axis=2, keepdims=False)
        v_own = lax.dynamic_index_in_dim(vb, own, axis=2, keepdims=False)
        s_sel = jnp.einsum('bhqd,bhqrpd->bhqrp', q_c, k_sel,
                           preferred_element_type=jnp.float32) * scale
        s_sel = jnp.where(valid_c[..., None], s_sel, -jnp.inf)
        s_sel = s_sel.reshape(B, H, MOBA_Q_CHUNK, n_sel * MOBA_BLOCK)
        q_pos = start + jnp.arange(MOBA_Q_CHUNK)
        k_pos = own * MOBA_BLOCK + jnp.arange(MOBA_BLOCK)
        s_own = jnp.einsum('bhqd,bhpd->bhqp', q_c, k_own,
                           preferred_element_type=jnp.float32) * scale
        s_own = jnp.where(k_pos[None, :] <= q_pos[:, None], s_own, -jnp.inf)
        p = jax.nn.softmax(jnp.concatenate([s_sel, s_own], axis=-1), axis=-1).astype(v.dtype)
        p_sel = p[..., :n_sel * MOBA_BLOCK].reshape(B, H, MOBA_Q_CHUNK, n_sel, MOBA_BLOCK)
        p_own = p[..., n_sel * MOBA_BLOCK:]
        return (jnp.einsum('bhqrp,bhqrpd->bhqd', p_sel, v_sel)
                + jnp.einsum('bhqp,bhpd->bhqd', p_own, v_own))

    starts = jnp.arange(nc, dtype=jnp.int32) * MOBA_Q_CHUNK
    out = lax.map(chunk_fn, (to_chunks(q), to_chunks(sel_idx), to_chunks(sel_valid), starts))
    return jnp.moveaxis(out, 0, 2).reshape(B, H, S, Dh)

def conformer_conv(a, gate, w, b, g, beta):
    u = a * jax.nn.sigmoid(gate)
    u = lax.conv_general_dilated(u, w[:, None, :], window_strides=(1,),
                                 padding=[(CONV_KERNEL - 1, 0)],
                                 dimension_numbers=('NWC', 'WIO', 'NWC'),
                                 feature_group_count=CONV_WIDTH) + b
    return jax.nn.silu(layer_norm(u, g, beta))

def peer_ffn(x, w_q, sub_keys, u_tab, v_tab):
    B, S, D = x.shape
    q = (x @ w_q).reshape(B, S, PEER_HEADS, 2, PEER_HALF)
    s = jnp.einsum('bshcd,hckd->bshck', q, sub_keys, preferred_element_type=jnp.float32)
    top_s, top_i = lax.top_k(s, PEER_TOPK)
    comb = top_s[..., 0, :, None] + top_s[..., 1, None, :]
    comb = comb.reshape(B, S, PEER_HEADS, PEER_TOPK * PEER_TOPK)
    best_s, best_c = lax.top_k(comb, PEER_TOPK)
    i1 = jnp.take_along_axis(top_i[..., 0, :], best_c // PEER_TOPK, axis=-1)
    i2 = jnp.take_along_axis(top_i[..., 1, :], best_c % PEER_TOPK, axis=-1)
    expert = (i1 * PEER_NKEYS + i2).reshape(B, S, PEER_HEADS * PEER_TOPK)
    gates = jax.nn.softmax(best_s, axis=-1).reshape(B, S, PEER_HEADS * PEER_TOPK).astype(x.dtype)

    nc = S // PEER_TOK_CHUNK

    def to_chunks(a):
        a = a.reshape(B, nc, PEER_TOK_CHUNK, *a.shape[2:])
        return jnp.moveaxis(a, 1, 0)

    def chunk_fn(args):
        x_c, e_c, g_c = args
        u = u_tab[e_c]
        h = jax.nn.gelu(jnp.einsum('bcd,bced->bce', x_c, u), approximate=False)
        return jnp.einsum('bce,bced->bcd', g_c * h, v_tab[e_c])

    y = lax.map(chunk_fn, (to_chunks(x), to_chunks(expert), to_chunks(gates)))
    return jnp.moveaxis(y, 0, 1).reshape(B, S, D)

def setup_inputs(seed: int = 0) -> dict:
    key = jax.random.key(seed)
    ks = jax.random.split(key, 16)
    f32 = jnp.float32
    x = jax.random.normal(ks[0], (BATCH, SEQ, D_MODEL), f32)
    col_scale = jnp.concatenate([
        jnp.ones((2 * ATTN_WIDTH,), f32),
        jnp.full((ATTN_WIDTH,), DEEPNORM_BETA, f32),
        jnp.ones((2 * CONV_WIDTH,), f32)])
    w_in = jax.random.normal(ks[1], (DEPTH, D_MODEL, MIX_IN), f32) * D_MODEL ** -0.5 * col_scale
    conv_w = jax.random.normal(ks[2], (DEPTH, CONV_KERNEL, CONV_WIDTH), f32) * CONV_KERNEL ** -0.5
    conv_b = 0.01 * jax.random.normal(ks[3], (DEPTH, CONV_WIDTH), f32)
    conv_ln_g = 1.0 + 0.01 * jax.random.normal(ks[4], (DEPTH, CONV_WIDTH), f32)
    conv_ln_b = 0.01 * jax.random.normal(ks[5], (DEPTH, CONV_WIDTH), f32)
    w_out = jax.random.normal(ks[6], (DEPTH, D_MODEL, D_MODEL), f32) * D_MODEL ** -0.5 * DEEPNORM_BETA
    ln1_g = 1.0 + 0.01 * jax.random.normal(ks[7], (DEPTH, D_MODEL), f32)
    ln1_b = 0.01 * jax.random.normal(ks[8], (DEPTH, D_MODEL), f32)
    peer_wq = jax.random.normal(ks[9], (DEPTH, D_MODEL, PEER_HEADS * PEER_QDIM), f32) * D_MODEL ** -0.5
    peer_keys = jax.random.normal(ks[10], (DEPTH, PEER_HEADS, 2, PEER_NKEYS, PEER_HALF), f32) * PEER_HALF ** -0.5
    peer_u = jax.random.normal(ks[11], (DEPTH, PEER_EXPERTS, D_MODEL), f32) * D_MODEL ** -0.5
    peer_v = jax.random.normal(ks[12], (DEPTH, PEER_EXPERTS, D_MODEL), f32) * DEEPNORM_BETA
    ln2_g = 1.0 + 0.01 * jax.random.normal(ks[13], (DEPTH, D_MODEL), f32)
    ln2_b = 0.01 * jax.random.normal(ks[14], (DEPTH, D_MODEL), f32)
    return {"x": x, "w_in": w_in, "conv_w": conv_w, "conv_b": conv_b,
            "conv_ln_g": conv_ln_g, "conv_ln_b": conv_ln_b, "w_out": w_out,
            "ln1_g": ln1_g, "ln1_b": ln1_b, "peer_wq": peer_wq, "peer_keys": peer_keys,
            "peer_u": peer_u, "peer_v": peer_v, "ln2_g": ln2_g, "ln2_b": ln2_b}

def reference(x, w_in, conv_w, conv_b, conv_ln_g, conv_ln_b, w_out, ln1_g, ln1_b,
              peer_wq, peer_keys, peer_u, peer_v, ln2_g, ln2_b):
    B, S, _ = x.shape
    cos, sin = rope_tables(S)
    cuts = [ATTN_WIDTH, 2 * ATTN_WIDTH, 3 * ATTN_WIDTH, 3 * ATTN_WIDTH + CONV_WIDTH]
    for l in range(DEPTH):
        proj = x @ w_in[l]
        q, k, v, a, g = jnp.split(proj, cuts, axis=-1)
        q = apply_rope(split_heads(q, B, S), cos, sin)
        k = apply_rope(split_heads(k, B, S), cos, sin)
        attn = moba_attention(q, k, split_heads(v, B, S))
        attn = attn.transpose(0, 2, 1, 3).reshape(B, S, ATTN_WIDTH)
        conv = conformer_conv(a, g, conv_w[l], conv_b[l], conv_ln_g[l], conv_ln_b[l])
        mixed = jnp.concatenate([attn, conv], axis=-1) @ w_out[l]
        x = layer_norm(DEEPNORM_ALPHA * x + mixed, ln1_g[l], ln1_b[l])
        ffn = peer_ffn(x, peer_wq[l], peer_keys[l], peer_u[l], peer_v[l])
        x = layer_norm(DEEPNORM_ALPHA * x + ffn, ln2_g[l], ln2_b[l])
    return x


_drawn_inputs = setup_inputs


def setup_inputs(seed=0):
    import zlib

    import numpy as np

    out = dict(_drawn_inputs(seed))
    spreads = {}
    factors = {'conv_b': 2.841, 'conv_ln_g': 3.419, 'conv_ln_b': 3.476}
    for name, (base, spread) in spreads.items():
        noise = np.random.default_rng([zlib.crc32(name.encode()), seed]).standard_normal(out[name].shape)
        drawn = base * np.exp(spread * noise) if base else spread * noise
        out[name] = __import__('jax').numpy.asarray(drawn.astype(out[name].dtype))
    for name, factor in factors.items():
        out[name] = (out[name] * factor).astype(out[name].dtype)
    return out
```

```python
from contextlib import ExitStack

import numpy as np
import concourse.bass as bass
from concourse import mybir

P = 128
SEQ, D, DEPTH = 256, 1024, 2
HEADS, DH = 8, 64
AW = HEADS * DH
CW = D - AW
TAPS = 31
PH, NK, TOPK = 8, 128, 16
HC = 2 * PH
ALPHA = (2 * DEPTH) ** 0.25
EPS = 1e-5
SCALE = DH ** -0.5
MASKED = -1e30
LOWEST = -3e38

TT = SEQ // P
KC = D // P
CT = CW // P
PAIRS = HEADS // 2
HALF = D // 2

AG0, QKV0 = 0, 2 * CT
WO0 = QKV0 + 3 * (KC // 2)
WQ0 = WO0 + KC
U0 = WQ0 + HC
V0 = U0 + NK
TILES = V0 + NK
RING = 4
HI_LEAD, LO_LEAD = 3, 2
WHI_LEAD, WLO_LEAD = 2, 1
GROUP = 4
GROUPS = SEQ // GROUP
TURNS = NK // RING
A_TURNS = PH
B_TURNS = PH
C_TURNS = PH
T_TURN = A_TURNS + B_TURNS + C_TURNS
LAST = TURNS - 1
DVE_STEPS = 542


class Signal:

    def __init__(self, ctx, nc, name, per_layer, unit=1, primed=0):
        self.sem = ctx.enter_context(nc.semaphore(name))
        self.per_layer, self.unit, self.primed = per_layer, unit, primed
        self.one = (self.sem, unit)

    def __call__(self, layer, k):
        return self.sem, (layer * self.per_layer + k + self.primed) * self.unit


class Steps:

    def __init__(self, engine, sem, base, per_turn):
        self.engine, self.sem, self.per_turn = engine, sem, per_turn
        self.base, self.n = base, 0

    def __call__(self, instruction):
        instruction.then_inc(self.sem, 1)
        self.n += 1
        return self.n

    def settle(self, n=None):
        self.engine.wait_ge(self.sem, self.base + (self.n if n is None else n))

    def settle_alone(self, held):
        self.settle()
        self.engine.sem_inc(held, 1)

    def turn(self, i, per_turn):
        return Steps(self.engine, self.sem, self.base + self.n + i * per_turn, per_turn)

    def ended(self, turn, turns=1):
        assert turn.n == turn.per_turn, (turn.n, turn.per_turn)
        self.n += turns * turn.n


def build(nc, x_in, stream, keys_t, conv_p, ln_p, rope, causal, out):
    f32, f32r, u32 = mybir.dt.float32, mybir.dt.float32r, mybir.dt.uint32
    ALU, ACT = mybir.AluOpType, mybir.ActivationFunctionType
    X = mybir.AxisListType.X
    ds = bass.ds

    ctx = ExitStack()
    with ctx:
        start = (nc.sbuf_base + 31) // 32 * 32
        used = [start]

        def place(name, shape, dt=f32, at=None):
            size = int(np.prod(shape[1:])) * 4
            if at is None:
                at = used[0]
                used[0] += size
            return nc.alloc_sbuf_tensor_at(name, shape, dt, offset=at)

        raw = place("raw", [P, RING, D])
        hi = place("hi", [P, RING, D], f32r)
        lo = place("lo", [P, RING, D], f32r)
        x = place("x", [P, TT, D])
        ident = place("ident", [P, P])
        iota = place("iota", [P, P])
        i1_t = place("i1_t", [P, SEQ])
        i2_t = place("i2_t", [P, SEQ])
        gate_hi = place("gate_hi", [P, SEQ], f32r)
        gate_lo = place("gate_lo", [P, SEQ], f32r)
        xt_at = used[0]
        xt = place("xt", [P, KC, 2, SEQ], f32r)
        ws = place("w_split", [P, RING, 2, SEQ], f32r, at=xt_at)
        one_a = place("onehot_a", [P, 2, GROUP, NK], at=xt_at)
        a_hi = place("gated_hi", [P, 2, GROUP, NK], f32r, at=xt_at + 4096)
        a_lo = place("gated_lo", [P, 2, GROUP, NK], f32r, at=xt_at + 8192)
        one_b = place("onehot_b", [P, 2, GROUP, NK], f32r, at=xt_at + 12288)
        ones = place("ones", [P, P])
        small = place("small", [P, 160])
        act = used[0]
        h = place("h", [P, NK * SEQ])
        assert used[0] <= nc.sbuf_top, used[0]
        h_tok = h[:, :].rearrange("p (b t) -> p t b", t=SEQ)

        def inside(name, at, shape, dt=f32):
            assert at + int(np.prod(shape[1:])) * 4 <= NK * SEQ * 4
            return place(name, shape, dt, at=act + at)

        ln2_g, ln2_b = inside("ln2_g", 0, [P, D]), inside("ln2_b", 4096, [P, D])
        ln1_g, ln1_b = inside("ln1_g", 8192, [P, D]), inside("ln1_b", 12288, [P, D])
        rope_sb = inside("rope_sb", 16384, [P, TT, 2, DH])
        causal_sb = inside("causal_sb", 17408, [P, 3 * P])
        conv_sb = inside("conv_sb", 18944, [P, CT, TAPS + 3])
        u_pad = inside("u_pad", 19968, [P, CT, 288])
        acc = inside("conv_acc", 24576, [P, CT, SEQ])
        xc = inside("conv_centred", 28672, [P, CT, SEQ])
        sq = inside("conv_squares", 32768, [P, CT, SEQ])
        sg = inside("sigmoid", 36864, [P, CT, SEQ])
        rstd = inside("conv_rstd", 40960, [P, 2, SEQ])
        q_sb = inside("q_rotated", 43008, [P, TT, AW])
        k_sb = inside("k_rotated", 47104, [P, TT, AW])
        m1, m2 = inside("rope_cos_part", 51200, [P, AW]), inside("rope_sin_part", 53248, [P, AW])
        v_sb = inside("v", 55296, [P, TT, AW])
        q_t = inside("q_t", 59392, [P, PAIRS, SEQ])
        k_t = inside("k_t", 63488, [P, PAIRS, SEQ])
        sm = inside("masked_scores", 67584, [P, HEADS, 3 * P])
        pr = inside("probs", 79872, [P, HEADS, 3 * P])
        p_t = inside("probs_t", 92160, [P, HEADS, 3 * P])
        mixed = inside("mixed", 104448, [P, KC, 2, SEQ], f32r)
        res = inside("residual", 120832, [P, TT, D])
        qp_t = inside("peer_q_t", 19968, [P, HC, SEQ])
        keys_sb = inside("keys_sb", 67584, [P, HC, NK])
        s_at = (T_TURN * RING) * SEQ * 4
        s_sb = inside("scores", s_at, [P, TT * HC * NK])
        t0 = s_at + TT * HC * NK * 4
        sg_in = inside("topk_in", t0, [P, 4, NK])
        sg_rest = inside("topk_rest", t0 + 2048, [P, 4, NK])
        top_v4 = inside("top_values_now", t0 + 4096, [P, 4, TOPK])
        top_i4 = inside("top_index_now", t0 + 4352, [P, 4, TOPK], u32)
        top_v = inside("top_values", t0 + 4608, [P, TT, HC, TOPK])
        top_i = inside("top_index", t0 + 6656, [P, TT, HC, TOPK])
        comb = inside("pair_sums", t0 + 8704, [P, TT, TOPK * TOPK])
        comb_rest = inside("pair_sums_rest", t0 + 10752, [P, TT, TOPK * TOPK])
        best_v2 = inside("best_values_now", t0 + 12800, [P, TT, TOPK])
        best_c2 = inside("best_places_now", t0 + 12928, [P, TT, TOPK], u32)
        best_v = inside("best_values", t0 + 13056, [P, TT, PH, TOPK])
        best_c = inside("best_places", t0 + 14080, [P, TT, PH, TOPK], u32)
        gate = inside("gates", t0 + 15104, [P, TT, PH, TOPK])
        gate_sum = inside("gate_sums", t0 + 16128, [P, TT, PH])
        gate_inv = inside("gate_inverses", t0 + 16192, [P, TT, PH])
        row_u = inside("row_place", t0, [P, TT, PH, TOPK], u32)
        col_u = inside("column_place", t0 + 1024, [P, TT, PH, TOPK], u32)
        row_f = inside("row_place_f", t0 + 2048, [P, TT, PH, TOPK])
        col_f = inside("column_place_f", t0 + 3072, [P, TT, PH, TOPK])
        e1 = inside("first_keys", s_at, [P, TT, PH, TOPK])
        e2 = inside("second_keys", s_at + 1024, [P, TT, PH, TOPK])

        cut = [0]

        def piece(n):
            cut[0] += n
            assert cut[0] <= 160
            return small[:, cut[0] - n:cut[0]]

        row_max, neg_max, row_sum, row_inv = piece(16), piece(16), piece(16), piece(16)
        ln_stats, ln_mv, ln_std, ln_rstd = piece(24), piece(4), piece(2), piece(2)

        bank = [ctx.enter_context(nc.psum_tensor(f"bank{n}", [P, 512], f32)) for n in range(8)]
        acc_banks = bank[0:4]
        ring_banks = bank[4:8]

        def signal(name, per_layer, unit=1, primed=0):
            return Signal(ctx, nc, name, per_layer, unit, primed)

        raw_in = [signal(f"raw_in{j}", TILES // RING, 16) for j in range(RING)]
        hi_done, lo_done = signal("hi_done", TILES), signal("lo_done", TILES)
        tile_used = signal("tile_used", TILES, primed=RING)
        x_loaded = signal("x_loaded", 1, 16)
        consts_made = signal("consts_made", 1)
        pool_setup = signal("pool_setup", 1)
        x_ready = signal("x_ready", TT, primed=TT)
        params_in = signal("params_in", 5, 16)
        keys_in = signal("keys_in", 1, 16)
        ln2_in = signal("ln2_params_in", 2, 16)
        xt_ps, xt_hi, xt_lo = signal("xt_ps", 8), signal("xt_hi", 8), signal("xt_lo", 8)
        sig_done, conv_u = signal("sigmoid_done", CT), signal("conv_u", CT)
        rotated, v_done = signal("rotated", 2 * TT), signal("v_done", TT)
        qk_ps, qk_done = signal("qk_t_ps", 4), signal("qk_t_done", 4)
        sc_ps, sc_used = signal("scores_ps", HEADS), signal("scores_masked", HEADS)
        max_done, exp_done = signal("max_done", HEADS), signal("exp_done", 2 * HEADS)
        pr_done, pt_ps = signal("probs_done", HEADS), signal("probs_t_ps", HEADS)
        pt_done, pv_ps = signal("probs_t_done", HEADS), signal("pv_ps", PAIRS)
        mix_hi, mix_lo = signal("mixed_hi", PAIRS + 1), signal("mixed_lo", PAIRS + 1)
        acc_done, mean_ps = signal("conv_done", 1), signal("conv_mean_ps", 1)
        centred, sq_done = signal("conv_centred_done", 1), signal("conv_squares_done", 1)
        var_ps, var_done = signal("conv_var_ps", 1), signal("conv_var_done", 1)
        std_done, normed = signal("conv_std_done", 1), signal("conv_normed", 1)
        silu_done = signal("silu_done", CT)
        ln_var, ln_root = signal("ln_var", 2 * TT), signal("ln_root", 2 * TT)
        x1_ready = signal("x1_ready", TT)
        qp_done, sp_ps = signal("peer_q_done", HC), signal("peer_scores_ps", TT * 4)
        s_done = signal("peer_scores_done", TT * 4)
        top_in, top_in_used = signal("topk_in_ready", A_TURNS), signal("topk_in_used", A_TURNS)
        best_done, gate_exp = signal("best_done", 1), signal("gate_exp", 1)
        chosen, chosen_ps = signal("chosen", 1), signal("chosen_t_ps", TT)
        tables = signal("chosen_tables", TT)
        gelu_done = signal("gelu_done", NK)
        one_done, gated_done = signal("onehots_done", GROUPS), signal("gated_done", GROUPS)
        g_ps, w_done = signal("gate_matrix_ps", GROUPS), signal("w_done", GROUPS)
        whi_done, wlo_done = signal("w_hi_done", NK), signal("w_lo_done", NK)
        out_done = signal("out_done", 1, 16)
        dve_held = ctx.enter_context(nc.semaphore("dve_held"))
        pool_held = ctx.enter_context(nc.semaphore("pool_held"))
        dve_steps = ctx.enter_context(nc.semaphore("dve_steps"))

        block = ctx.enter_context(nc.Block())

        @block.sync
        def _(sp):
            for t in range(TT):
                sp.dma_start(x[:, t, :], x_in[t * P:(t + 1) * P, :]).then_inc(*x_loaded.one)
            for j in range(RING):
                sp.dma_start(raw[:, j, :], stream[j * P:(j + 1) * P, :]).then_inc(*raw_in[j].one)
            with sp.Fori(1, DEPTH * TILES // RING) as turn:
                for j in range(RING):
                    sp.wait_ge(*lo_done(0, RING * turn + (j - RING + 1)))
                    sp.dma_start(raw[:, j, :], stream[ds((RING * turn + j) * P, P), :])\
                      .then_inc(*raw_in[j].one)
            sp.wait_ge(*x_ready(DEPTH - 1, TT))
            for t in range(TT):
                sp.dma_start(out[t * P:(t + 1) * P, :], x[:, t, :]).then_inc(*out_done.one)
            sp.wait_ge(*out_done(0, TT))

        @block.gpsimd
        def _(pool):
            nc.gpsimd.iota(iota[:, :], pattern=[[1, P]], base=0, channel_multiplier=0,
                           allow_small_or_imprecise_dtypes=True)
            nc.gpsimd.memset(ones[:, :], 1.0 / CW)
            nc.gpsimd.memset(ident[:, :], 0.0).then_inc(*pool_setup.one)
            pool.wait_ge(*pool_setup(0, 1))
            nc.gpsimd.affine_select(out=ident[:, :], in_=ident[:, :], compare_op=ALU.not_equal,
                                    fill=1.0, base=0, pattern=[[-1, P]], channel_multiplier=1)\
              .then_inc(*consts_made.one)
            with pool.Fori(0, DEPTH) as layer:
                pool.wait_ge(*s_done(layer, TT * 4))
                pool.sem_inc(pool_held, 1)
                nc.gpsimd.tensor_copy(sg_in[:, :, :], s_sb[:, 0:4 * NK]).then_inc(*top_in.one)
                with pool.Fori(1, A_TURNS) as i:
                    pool.wait_ge(*top_in_used(layer, i))
                    pool.sem_inc(pool_held, 1)
                    nc.gpsimd.tensor_copy(sg_in[:, :, :], s_sb[:, ds(i * (4 * NK), 4 * NK)])\
                      .then_inc(*top_in.one)
                with pool.Fori(0, GROUPS // 2) as i:
                    for b in range(2):
                        pool.wait_ge(*one_done(layer, 2 * i + (b + 1)))
                        tok = ds(i * (2 * GROUP) + b * GROUP, GROUP)
                        nc.gpsimd.tensor_tensor(
                            a_hi[:, b], one_a[:, b],
                            gate_hi[:, tok].bitcast(f32)[:, :, None].to_broadcast([P, GROUP, NK]),
                            ALU.mult)
                        nc.gpsimd.tensor_tensor(
                            a_lo[:, b], one_a[:, b],
                            gate_lo[:, tok].bitcast(f32)[:, :, None].to_broadcast([P, GROUP, NK]),
                            ALU.mult).then_inc(*gated_done.one)

        @block.scalar
        def _(act):
            act.wait_ge(*consts_made(0, 1))
            with act.Fori(0, DEPTH) as layer:

                def head(turn, j):
                    turn, j = turn + j // RING, j % RING
                    act.wait_ge(*raw_in[j](layer, turn + 1))
                    act.wait_ge(*tile_used(layer, RING * turn + (j - RING + 1)))
                    nc.scalar.activation(hi[:, j, :], raw[:, j, :], ACT.Copy).then_inc(*hi_done.one)

                def x_heads(done):
                    for c in range(4):
                        act.wait_ge(*xt_ps(layer, done + c + 1))
                        nc.scalar.activation(
                            xt[:, 2 * c:2 * c + 2, 0, :],
                            ring_banks[c][:, :].rearrange("p (k t) -> p k t", k=2), ACT.Copy)\
                          .then_inc(*xt_hi.one)

                act.wait_ge(*x_ready(layer, 0))
                act.dma_start(conv_sb[:, :, :], conv_p[ds(layer * P, P), :])\
                   .then_inc(*params_in.one)
                act.dma_start(rope_sb[:, :, :, :], rope).then_inc(*params_in.one)
                act.dma_start(causal_sb[:, :], causal).then_inc(*params_in.one)
                act.dma_start(ln1_g[:, :], ln_p[ds(layer * 4, 1), :].to_broadcast([P, D]))\
                   .then_inc(*params_in.one)
                act.dma_start(ln1_b[:, :], ln_p[ds(layer * 4 + 1, 1), :].to_broadcast([P, D]))\
                   .then_inc(*params_in.one)
                for n in range(HI_LEAD):
                    head(0, n)
                x_heads(0)
                for n in range(AG0, QKV0):
                    head(0, n + HI_LEAD)
                    if n % 2:
                        act.wait_ge(*tile_used(layer, n + 1))
                        nc.scalar.activation(sg[:, n // 2, :], bank[(4 + n) % 8][:, 0:SEQ],
                                             ACT.Sigmoid).then_inc(*sig_done.one)
                for n in range(QKV0, WO0):
                    head(0, n + HI_LEAD)
                act.wait_ge(*tile_used(layer, WO0))
                for t in range(TT):
                    nc.scalar.activation(v_sb[:, t, :], bank[t][:, :], ACT.Copy)\
                      .then_inc(*v_done.one)
                for c, (dst, b) in enumerate(((q_t, 2), (q_t, 3), (k_t, 4), (k_t, 5))):
                    act.wait_ge(*qk_ps(layer, c + 1))
                    nc.scalar.activation(dst[:, 2 * (c % 2):2 * (c % 2) + 2, :],
                                         bank[b][:, :].rearrange("p (k t) -> p k t", k=2),
                                         ACT.Copy).then_inc(*qk_done.one)
                def probs_transposed(g):
                    act.wait_ge(*pt_ps(layer, g + 1))
                    nc.scalar.activation(p_t[:, g, :], bank[4 + g % 2][:, 0:3 * P], ACT.Copy)\
                      .then_inc(*pt_done.one)

                def pv_heads(pair):
                    act.wait_ge(*pv_ps(layer, pair + 1))
                    nc.scalar.activation(mixed[:, pair, 0, :], bank[pair % 2][:, 0:SEQ], ACT.Copy)\
                      .then_inc(*mix_hi.one)

                for g in range(HEADS):
                    act.wait_ge(*max_done(layer, g + 1))
                    for t, (c0, c1) in enumerate(((0, P), (P, 3 * P))):
                        nc.scalar.activation(pr[:, g, c0:c1], sm[:, g, c0:c1], ACT.Exp,
                                             bias=neg_max[:, 2 * g + t:2 * g + t + 1], scale=SCALE,
                                             accum_out=row_sum[:, 2 * g + t:2 * g + t + 1])\
                          .then_inc(*exp_done.one)
                    if g == 1:
                        act.wait_ge(*centred(layer, 1))
                        nc.scalar.activation(sq[:, :, :], xc[:, :, :], ACT.Square)\
                          .then_inc(*sq_done.one)
                    if g >= 2:
                        probs_transposed(g - 2)
                    if g >= 4 and g % 2 == 0:
                        pv_heads(g // 2 - 2)
                for g in range(HEADS - 2, HEADS):
                    probs_transposed(g)
                act.wait_ge(*var_done(layer, 1))
                nc.scalar.activation(rstd[:, 0, :], rstd[:, 1, :], ACT.Sqrt)\
                  .then_inc(*std_done.one)
                act.wait_ge(*params_in(layer, 5))
                act.wait_ge(*normed(layer, 1))
                for c in range(CT):
                    nc.scalar.activation(sq[:, c, :], xc[:, c, :], ACT.Silu,
                                         bias=conv_sb[:, c, TAPS + 2:TAPS + 3],
                                         scale=conv_sb[:, c, TAPS + 1:TAPS + 2])\
                      .then_inc(*silu_done.one)
                for pair in range(PAIRS - 2, PAIRS):
                    pv_heads(pair)
                act.wait_ge(*silu_done(layer, CT))
                nc.scalar.activation(mixed[:, PAIRS:KC, 0, :], sq[:, :, :], ACT.Copy)\
                  .then_inc(*mix_hi.one)
                act.wait_ge(*pt_ps(layer, HEADS))
                act.dma_start(keys_sb[:, :, :], keys_t[ds(layer * P, P), :]).then_inc(*keys_in.one)
                for n in range(WO0, WQ0):
                    head(0, n + HI_LEAD)
                for t in range(TT):
                    act.wait_ge(*ln_var(layer, t + 1))
                    nc.scalar.activation(ln_std[:, t:t + 1], ln_mv[:, 2 * t + 1:2 * t + 2], ACT.Sqrt)\
                      .then_inc(*ln_root.one)
                x_heads(4)
                for n in range(WQ0, U0):
                    head(0, n + HI_LEAD)
                    act.wait_ge(*tile_used(layer, n + 1))
                    nc.scalar.activation(qp_t[:, n - WQ0, :], bank[n % 8][:, 0:SEQ], ACT.Copy)\
                      .then_inc(*qp_done.one)
                for c in range(TT * 4):
                    act.wait_ge(*sp_ps(layer, c + 1))
                    nc.scalar.activation(s_sb[:, c * 512:(c + 1) * 512], bank[c][:, :], ACT.Copy)\
                      .then_inc(*s_done.one)

                def u_turn(i):
                    for j in range(RING):
                        head(i + U0 // RING, j + HI_LEAD)
                        act.wait_ge(*tile_used(layer, RING * i + (U0 + j + 1)))
                        nc.scalar.activation(h[:, ds(i * (RING * SEQ) + j * SEQ, SEQ)],
                                             ring_banks[j][:, 0:SEQ], ACT.Gelu)\
                          .then_inc(*gelu_done.one)

                with act.Fori(0, A_TURNS + B_TURNS) as i:
                    u_turn(i)
                act.wait_ge(*best_done(layer, 1))
                nc.scalar.activation(gate[:, :, :, :], gate[:, :, :, :], ACT.Exp)\
                  .then_inc(*gate_exp.one)
                with act.Fori(A_TURNS + B_TURNS, T_TURN) as i:
                    u_turn(i)
                act.wait_ge(*tables(layer, TT))
                with act.Fori(T_TURN, TURNS) as i:
                    u_turn(i)

                def w_head(i, j):
                    i, j = i + j // RING, j % RING
                    act.wait_ge(*tile_used(layer, RING * i + (V0 + j - RING + 1)))
                    nc.scalar.activation(ws[:, j, 0, :], h[:, ds(i * (RING * SEQ) + j * SEQ, SEQ)],
                                         ACT.Copy).then_inc(*whi_done.one)

                def v_turn(i):
                    for j in range(RING):
                        w_head(i, j + WHI_LEAD)
                        head(i + V0 // RING, j + HI_LEAD)

                act.wait_ge(*w_done(layer, GROUPS))
                for b in range(WHI_LEAD):
                    w_head(0, b)
                with act.Fori(0, TURNS // 2) as i:
                    v_turn(i)
                act.wait_ge(*wlo_done(layer, NK // 2))
                act.dma_start(ln2_g[:, :], ln_p[ds(layer * 4 + 2, 1), :].to_broadcast([P, D]))\
                   .then_inc(*ln2_in.one)
                act.dma_start(ln2_b[:, :], ln_p[ds(layer * 4 + 3, 1), :].to_broadcast([P, D]))\
                   .then_inc(*ln2_in.one)
                with act.Fori(TURNS // 2, LAST) as i:
                    v_turn(i)
                for j in range(RING):
                    if j + WHI_LEAD < RING:
                        w_head(LAST, j + WHI_LEAD)
                    if j + HI_LEAD < RING:
                        head(LAST + V0 // RING, j + HI_LEAD)
                for t in range(TT):
                    act.wait_ge(*ln_var(layer, TT + t + 1))
                    nc.scalar.activation(ln_std[:, t:t + 1], ln_mv[:, 2 * t + 1:2 * t + 2], ACT.Sqrt)\
                      .then_inc(*ln_root.one)

        @block.vector
        def _(dve):
            vec = nc.vector
            dve.wait_ge(*x_loaded(0, TT))
            dve.wait_ge(*consts_made(0, 1))
            for t in range(TT):
                dve.sem_inc(*x_ready.one)
            with dve.Fori(0, DEPTH) as layer:
                step = Steps(dve, dve_steps, layer * DVE_STEPS, DVE_STEPS)

                def rest(turn, j):
                    turn, j = turn + j // RING, j % RING
                    dve.wait_ge(*hi_done(layer, RING * turn + (j + 1)))
                    vec.tensor_tensor(lo[:, j, :], raw[:, j, :], hi[:, j, :].bitcast(f32),
                                      ALU.subtract).then_inc(*lo_done.one)

                def x_rests(done):
                    for c in range(4):
                        dve.wait_ge(*xt_hi(layer, done + c + 1))
                        vec.tensor_tensor(xt[:, 2 * c:2 * c + 2, 1, :],
                                          ring_banks[c][:, :].rearrange("p (k t) -> p k t", k=2),
                                          xt[:, 2 * c:2 * c + 2, 0, :].bitcast(f32),
                                          ALU.subtract).then_inc(*xt_lo.one)

                def layer_norm(which, t, gain, shift, last):
                    for c in range(2):
                        step(vec.scalar_tensor_tensor(
                            res[:, t, c * HALF:(c + 1) * HALF], x[:, t, c * HALF:(c + 1) * HALF],
                            ALPHA, acc_banks[2 * t + c][:, :], ALU.mult, ALU.add))
                    step.settle()
                    for c in range(2):
                        step(vec.bn_stats(ln_stats[:, 12 * t + 6 * c:12 * t + 6 * c + 6],
                                          res[:, t, c * HALF:(c + 1) * HALF]))
                    step.settle_alone(dve_held)
                    mean, var = ln_mv[:, 2 * t:2 * t + 1], ln_mv[:, 2 * t + 1:2 * t + 2]
                    step(vec.bn_aggr(ln_mv[:, 2 * t:2 * t + 2], ln_stats[:, 12 * t:12 * t + 12]))
                    step.settle()
                    vec.tensor_scalar_add(var, var, EPS).then_inc(*ln_var.one)
                    dve.wait_ge(*ln_root(layer, TT * which + t + 1))
                    step(vec.reciprocal(ln_rstd[:, t:t + 1], ln_std[:, t:t + 1]))
                    step.settle()
                    step(vec.tensor_scalar(res[:, t, :], res[:, t, :], mean, ln_rstd[:, t:t + 1],
                                           ALU.subtract, ALU.mult))
                    step.settle()
                    step(vec.tensor_tensor(res[:, t, :], res[:, t, :], gain[:, :], ALU.mult))
                    step.settle()
                    vec.tensor_tensor(x[:, t, :], res[:, t, :], shift[:, :], ALU.add)\
                       .then_inc(*last.one)

                for n in range(LO_LEAD):
                    rest(0, n)
                step(vec.memset(u_pad[:, :, 0:TAPS - 1], 0.0))
                x_rests(0)
                for n in range(AG0, QKV0):
                    rest(0, n + LO_LEAD)
                    if n % 2:
                        dve.wait_ge(*sig_done(layer, n // 2 + 1))
                        vec.tensor_tensor(u_pad[:, n // 2, TAPS - 1:TAPS - 1 + SEQ],
                                          bank[(3 + n) % 8][:, 0:SEQ], sg[:, n // 2, :],
                                          ALU.mult).then_inc(*conv_u.one)
                dve.wait_ge(*conv_u(layer, CT))
                dve.wait_ge(*params_in(layer, 5))

                def taps(first, last):
                    for tap in range(first, last):
                        for c in range(CT):
                            window = u_pad[:, c, tap:tap + SEQ]
                            weight = conv_sb[:, c, tap:tap + 1]
                            if tap == 0:
                                step(vec.tensor_scalar(acc[:, c, :], window, weight,
                                                       conv_sb[:, c, TAPS:TAPS + 1],
                                                       ALU.mult, ALU.add))
                            else:
                                step.settle(step.n - CT + 1)
                                step(vec.scalar_tensor_tensor(acc[:, c, :], window, weight,
                                                              acc[:, c, :], ALU.mult, ALU.add))

                def rotate(banks, dst, before):
                    for t in range(TT):
                        if before + t:
                            dve.wait_ge(*rotated(layer, before + t))
                        src = banks[t][:, :].rearrange("p (h a d) -> p h a d", a=2, d=DH // 2)
                        cos = rope_sb[:, t, 0, :][:, None, :].to_broadcast([P, HEADS, DH])
                        sin = rope_sb[:, t, 1, :].rearrange("p (a d) -> p a d", a=2)
                        m2v = m2[:, :].rearrange("p (h a d) -> p h a d", a=2, d=DH // 2)
                        step(vec.tensor_tensor(m1[:, :].rearrange("p (h d) -> p h d", d=DH),
                                               banks[t][:, :].rearrange("p (h d) -> p h d", d=DH),
                                               cos, ALU.mult))
                        for a in range(2):
                            step(vec.tensor_tensor(
                                m2v[:, :, a, :], src[:, :, 1 - a, :],
                                sin[:, a, :][:, None, :].to_broadcast([P, HEADS, DH // 2]),
                                ALU.mult))
                        step.settle()
                        vec.tensor_tensor(dst[:, t, :], m1[:, :], m2[:, :], ALU.add)\
                           .then_inc(*rotated.one)

                n_qkv = WO0 - QKV0
                for n in range(n_qkv):
                    rest(0, QKV0 + n + LO_LEAD)
                    taps(TAPS * n // n_qkv, TAPS * (n + 1) // n_qkv)
                    if n == 5:
                        dve.wait_ge(*tile_used(layer, QKV0 + 4))
                        rotate(bank[4:6], q_sb, 0)
                    if n == 9:
                        dve.wait_ge(*tile_used(layer, QKV0 + 8))
                        rotate(bank[6:8], k_sb, TT)
                step.settle()
                dve.sem_inc(*acc_done.one)

                def mask_and_max(g):
                    dve.wait_ge(*sc_ps(layer, g + 1))
                    vec.tensor_tensor(sm[:, g, :], bank[6 + g % 2][:, 0:3 * P], causal_sb[:, :],
                                      ALU.add).then_inc(*sc_used.one)
                    dve.wait_ge(*sc_used(layer, g + 1))
                    for t, (c0, c1) in enumerate(((0, P), (P, 3 * P))):
                        step(vec.reduce_max(row_max[:, 2 * g + t:2 * g + t + 1], sm[:, g, c0:c1], X))
                    step.settle()
                    vec.tensor_scalar(neg_max[:, 2 * g:2 * g + 2], row_max[:, 2 * g:2 * g + 2],
                                      -SCALE, None, ALU.mult).then_inc(*max_done.one)

                def normalise(g):
                    dve.wait_ge(*exp_done(layer, 2 * g + 2))
                    step(vec.reciprocal(row_inv[:, 2 * g:2 * g + 2], row_sum[:, 2 * g:2 * g + 2]))
                    step.settle()
                    step(vec.tensor_scalar(pr[:, g, 0:P], pr[:, g, 0:P],
                                           row_inv[:, 2 * g:2 * g + 1], None, ALU.mult))
                    vec.tensor_scalar(pr[:, g, P:3 * P], pr[:, g, P:3 * P],
                                      row_inv[:, 2 * g + 1:2 * g + 2], None, ALU.mult)\
                       .then_inc(*pr_done.one)

                def pv_rests(pair):
                    dve.wait_ge(*mix_hi(layer, pair + 1))
                    vec.tensor_tensor(mixed[:, pair, 1, :], bank[pair % 2][:, 0:SEQ],
                                      mixed[:, pair, 0, :].bitcast(f32), ALU.subtract)\
                       .then_inc(*mix_lo.one)

                mask_and_max(0)
                mask_and_max(1)
                dve.wait_ge(*mean_ps(layer, 1))
                vec.tensor_tensor(xc[:, :, :], acc[:, :, :],
                                  bank[3][:, None, 0:SEQ].to_broadcast([P, CT, SEQ]),
                                  ALU.subtract).then_inc(*centred.one)
                for g in range(HEADS):
                    normalise(g)
                    if g + 2 < HEADS:
                        mask_and_max(g + 2)
                    if g == 3:
                        dve.wait_ge(*var_ps(layer, 1))
                        vec.tensor_scalar(rstd[:, 1, :], bank[2][:, 0:SEQ], EPS, None, ALU.add)\
                           .then_inc(*var_done.one)
                    if g >= 4 and g % 2 == 0:
                        pv_rests(g // 2 - 2)
                dve.wait_ge(*std_done(layer, 1))
                step(vec.reciprocal(rstd[:, 1, :], rstd[:, 0, :]))
                step.settle()
                dve.wait_ge(*centred(layer, 1))
                dve.wait_ge(*sq_done(layer, 1))
                vec.tensor_tensor(xc[:, :, :], xc[:, :, :],
                                  rstd[:, 1:2, :].to_broadcast([P, CT, SEQ]), ALU.mult)\
                   .then_inc(*normed.one)
                for pair in range(PAIRS - 2, PAIRS):
                    pv_rests(pair)
                dve.wait_ge(*mix_hi(layer, PAIRS + 1))
                vec.tensor_tensor(mixed[:, PAIRS:KC, 1, :], sq[:, :, :],
                                  mixed[:, PAIRS:KC, 0, :].bitcast(f32), ALU.subtract)\
                   .then_inc(*mix_lo.one)

                for n in range(WO0, WQ0):
                    rest(0, n + LO_LEAD)
                dve.wait_ge(*tile_used(layer, WQ0))
                for t in range(TT):
                    layer_norm(0, t, ln1_g, ln1_b, x1_ready)
                x_rests(4)
                for n in range(WQ0, U0):
                    rest(0, n + LO_LEAD)

                def u_rests(i):
                    for j in range(RING):
                        rest(i + U0 // RING, j + LO_LEAD)

                def top16(values, index, src, spare, m, now):
                    for r in range(2):
                        this = src if r == 0 else spare
                        low = slice(8 * r, 8 * r + 8)
                        for g in range(m):
                            now(vec.max(values[:, g, low], this[:, g, :]))
                        now.settle_alone(dve_held)
                        for g in range(m):
                            if r == 0:
                                now(vec.match_replace(spare[:, g, :], values[:, g, low],
                                                      this[:, g, :], LOWEST))
                            now(vec.max_index(index[:, g, low], values[:, g, low], this[:, g, :]))
                        now.settle_alone(dve_held)

                A_STEPS = 22
                with dve.Fori(0, A_TURNS) as i:
                    now = step.turn(i, A_STEPS)
                    u_rests(i)
                    dve.wait_ge(*top_in(layer, i + 1))
                    dve.sem_inc(dve_held, 1)
                    top16(top_v4, top_i4, sg_in, sg_rest, 4, now)
                    dve.sem_inc(*top_in_used.one)
                    now(vec.tensor_copy(
                        top_v[:, :, :, :].rearrange("p t g k -> p (t g k)")[:, ds(i * 64, 64)],
                        top_v4[:, :, :].rearrange("p g k -> p (g k)")))
                    now(vec.tensor_copy(
                        top_i[:, :, :, :].rearrange("p t g k -> p (t g k)")[:, ds(i * 64, 64)],
                        top_i4[:, :, :].rearrange("p g k -> p (g k)")))
                    now.settle_alone(dve_held)
                step.ended(now, A_TURNS)

                B_STEPS = 13
                top_v_flat = top_v[:, :, :, :].rearrange("p t g k -> p t (g k)")
                best_v_flat = best_v[:, :, :, :].rearrange("p t g k -> p t (g k)")
                best_c_flat = best_c[:, :, :, :].rearrange("p t g k -> p t (g k)")
                with dve.Fori(0, B_TURNS) as i:
                    now = step.turn(i, B_STEPS)
                    u_rests(i + A_TURNS)
                    first = top_v_flat[:, :, ds(i * (2 * TOPK), TOPK)]
                    second = top_v_flat[:, :, ds(i * (2 * TOPK) + TOPK, TOPK)]
                    now(vec.tensor_tensor(
                        comb[:, :, :].rearrange("p t (a b) -> p t a b", a=TOPK),
                        first[:, :, :, None].to_broadcast([P, TT, TOPK, TOPK]),
                        second[:, :, None, :].to_broadcast([P, TT, TOPK, TOPK]), ALU.add))
                    now.settle_alone(dve_held)
                    top16(best_v2, best_c2, comb, comb_rest, TT, now)
                    now(vec.tensor_copy(best_v_flat[:, :, ds(i * TOPK, TOPK)], best_v2[:, :, :]))
                    now(vec.tensor_copy(best_c_flat[:, :, ds(i * TOPK, TOPK)], best_c2[:, :, :]))
                    now.settle()
                step.ended(now, B_TURNS)
                vec.tensor_tensor(gate[:, :, :, :].rearrange("p t g k -> p (t g) k"),
                                  best_v[:, :, :, :].rearrange("p t g k -> p (t g) k"),
                                  best_v[:, :, :, 0:1].rearrange("p t g k -> p (t g) k")
                                  .to_broadcast([P, TT * PH, TOPK]),
                                  ALU.subtract).then_inc(*best_done.one)
                step(vec.tensor_scalar(row_u[:, :, :, :], best_c[:, :, :, :], 4, None,
                                       ALU.logical_shift_right))
                step(vec.tensor_scalar(col_u[:, :, :, :], best_c[:, :, :, :], 15, None,
                                       ALU.bitwise_and))
                step.settle()
                step(vec.tensor_copy(row_f[:, :, :, :], row_u[:, :, :, :]))
                step(vec.tensor_copy(col_f[:, :, :, :], col_u[:, :, :, :]))
                step.settle_alone(dve_held)

                C_STEPS = 6
                with dve.Fori(0, C_TURNS) as i:
                    now = step.turn(i, C_STEPS)
                    u_rests(i + A_TURNS + B_TURNS)
                    number = iota[:, 0:TOPK][:, None, None, :].to_broadcast([P, TT, TOPK, TOPK])
                    cmp = comb[:, :, :].rearrange("p t (a b) -> p t a b", a=TOPK)
                    hit = comb_rest[:, :, :].rearrange("p t (a b) -> p t a b", a=TOPK)
                    top_i_flat = top_i[:, :, :, :].rearrange("p t g k -> p t (g k)")
                    for half, (place_f, dst) in enumerate(((row_f, e1), (col_f, e2))):
                        here = place_f[:, :, :, :].rearrange("p t g k -> p t (g k)")[
                            :, :, ds(i * TOPK, TOPK)]
                        keys = top_i_flat[:, :, ds(i * (2 * TOPK) + half * TOPK, TOPK)]
                        now(vec.tensor_tensor(
                            cmp, here[:, :, :, None].to_broadcast([P, TT, TOPK, TOPK]), number,
                            ALU.is_equal))
                        now.settle()
                        now(vec.tensor_tensor(
                            hit, cmp, keys[:, :, None, :].to_broadcast([P, TT, TOPK, TOPK]),
                            ALU.mult))
                        now.settle()
                        now(vec.tensor_reduce(
                            dst[:, :, :, :].rearrange("p t g k -> p t (g k)")[
                                :, :, ds(i * TOPK, TOPK)], hit, X, ALU.add))
                    now.settle()
                step.ended(now, C_TURNS)
                dve.wait_ge(*gate_exp(layer, 1))
                step(vec.tensor_reduce(gate_sum[:, :, :].rearrange("p t g -> p (t g)"),
                                       gate[:, :, :, :].rearrange("p t g k -> p (t g) k"), X,
                                       ALU.add))
                step.settle()
                step(vec.reciprocal(gate_inv[:, :, :], gate_sum[:, :, :]))
                step.settle()
                vec.tensor_tensor(gate[:, :, :, :].rearrange("p t g k -> p (t g) k"),
                                  gate[:, :, :, :].rearrange("p t g k -> p (t g) k"),
                                  gate_inv[:, :, :].rearrange("p t g -> p (t g)")[:, :, None]
                                  .to_broadcast([P, TT * PH, TOPK]), ALU.mult)\
                   .then_inc(*chosen.one)
                for t in range(TT):
                    tok = slice(t * P, (t + 1) * P)
                    dve.wait_ge(*chosen_ps(layer, t + 1))
                    step(vec.tensor_copy(i1_t[:, tok], bank[t][:, 0:P]))
                    step(vec.tensor_copy(i2_t[:, tok], bank[t][:, P:2 * P]))
                    step(vec.tensor_copy(gate_hi[:, tok], bank[t][:, 2 * P:3 * P]))
                    step.settle()
                    vec.tensor_tensor(gate_lo[:, tok], bank[t][:, 2 * P:3 * P],
                                      gate_hi[:, tok].bitcast(f32), ALU.subtract)\
                       .then_inc(*tables.one)
                with dve.Fori(T_TURN, TURNS) as i:
                    u_rests(i)

                def one_hots(i, b):
                    i, b = i + b // 2, b % 2
                    tok = ds(i * (2 * GROUP) + b * GROUP, GROUP)
                    number = iota[:, None, :].to_broadcast([P, GROUP, NK])
                    vec.tensor_tensor(one_a[:, b], number,
                                      i1_t[:, tok][:, :, None].to_broadcast([P, GROUP, NK]),
                                      ALU.is_equal)
                    vec.tensor_tensor(one_b[:, b], number,
                                      i2_t[:, tok][:, :, None].to_broadcast([P, GROUP, NK]),
                                      ALU.is_equal).then_inc(*one_done.one)

                def gate_block(i, b):
                    dve.wait_ge(*g_ps(layer, 2 * i + (b + 1)))
                    here = h_tok[:, ds(i * (2 * GROUP) + b * GROUP, GROUP), :]
                    vec.tensor_tensor(here,
                                      ring_banks[b][:, :].rearrange("p (t b) -> p t b", b=NK),
                                      here, ALU.mult).then_inc(*w_done.one)

                dve.wait_ge(*tables(layer, TT))
                dve.wait_ge(*tile_used(layer, V0))
                one_hots(0, 0)
                one_hots(0, 1)
                dve.wait_ge(*gelu_done(layer, NK))
                dve.sem_inc(dve_held, 1)
                with dve.Fori(0, GROUPS // 2 - 1) as i:
                    for b in range(2):
                        gate_block(i, b)
                        one_hots(i, b + 2)
                for b in range(2):
                    gate_block(GROUPS // 2 - 1, b)

                def w_rest(i, j):
                    i, j = i + j // RING, j % RING
                    dve.wait_ge(*whi_done(layer, RING * i + (j + 1)))
                    vec.tensor_tensor(ws[:, j, 1, :], h[:, ds(i * (RING * SEQ) + j * SEQ, SEQ)],
                                      ws[:, j, 0, :].bitcast(f32), ALU.subtract)\
                       .then_inc(*wlo_done.one)

                for b in range(WLO_LEAD):
                    w_rest(0, b)
                with dve.Fori(0, LAST) as i:
                    for j in range(RING):
                        w_rest(i, j + WLO_LEAD)
                        rest(i + V0 // RING, j + LO_LEAD)
                for j in range(RING):
                    if j + WLO_LEAD < RING:
                        w_rest(LAST, j + WLO_LEAD)
                    if j + LO_LEAD < RING:
                        rest(LAST + V0 // RING, j + LO_LEAD)
                dve.wait_ge(*tile_used(layer, TILES))
                dve.wait_ge(*ln2_in(layer, 2))
                for t in range(TT):
                    layer_norm(1, t, ln2_g, ln2_b, x_ready)
                assert step.n == DVE_STEPS, step.n

        @block.tensor
        def _(pe):
            mm = nc.tensor.matmul
            for _ in range(RING):
                pe.sem_inc(tile_used.sem, 1)
            pe.wait_ge(*consts_made(0, 1))
            with pe.Fori(0, DEPTH) as layer:

                def transpose_x():
                    for c in range(4):
                        for k in range(2):
                            for t in range(TT):
                                last = nc.tensor.transpose(
                                    ring_banks[c][:, k * SEQ + t * P:k * SEQ + (t + 1) * P],
                                    x[:, t, (2 * c + k) * P:(2 * c + k + 1) * P], ident[:, :])
                        last.then_inc(*xt_ps.one)

                def tile_by_x(slot, dst):
                    for k in range(KC):
                        w_hi, w_lo = hi[:, slot, k * P:(k + 1) * P], lo[:, slot, k * P:(k + 1) * P]
                        mm(dst, w_hi, xt[:, k, 0, :], start=k == 0, stop=False)
                        mm(dst, w_hi, xt[:, k, 1, :], start=False, stop=False)
                        last = mm(dst, w_lo, xt[:, k, 0, :], start=False, stop=k == KC - 1)
                    last.then_inc(*tile_used.one)

                def by_tile(slot, stationary, chunks, banks, first, final):
                    for t in range(TT):
                        for n, (k, col, c) in enumerate(chunks):
                            dst = banks[t][c][:, :]
                            begin = first and n < len(banks[t])
                            end = final and n >= len(chunks) - len(banks[t])
                            cols = slice(col, col + HALF)
                            mm(dst, stationary(0, t, k), hi[:, slot, cols], start=begin, stop=False)
                            mm(dst, stationary(0, t, k), lo[:, slot, cols], start=False, stop=False)
                            last = mm(dst, stationary(1, t, k), hi[:, slot, cols], start=False,
                                      stop=end)
                    last.then_inc(*tile_used.one)

                def x_part(part, t, k):
                    return xt[:, k, part, t * P:(t + 1) * P]

                def mixed_part(part, t, k):
                    return mixed[:, k, part, t * P:(t + 1) * P]

                model_banks = [[acc_banks[2 * t], acc_banks[2 * t + 1]] for t in range(TT)]

                pe.wait_ge(*x_ready(layer, 0))
                transpose_x()
                pe.wait_ge(*xt_lo(layer, 4))
                for n in range(AG0, QKV0):
                    pe.wait_ge(*lo_done(layer, n + 1))
                    tile_by_x(n % RING, bank[(4 + n) % 8][:, 0:SEQ])
                for g, (b, used_by) in enumerate(((4, 1), (6, 2), (0, 3))):
                    pe.wait_ge(*conv_u(layer, used_by))
                    for m in range(4):
                        n = QKV0 + 4 * g + m
                        pe.wait_ge(*lo_done(layer, n + 1))
                        by_tile(n % RING, x_part, [(2 * m, 0, 0), (2 * m + 1, HALF, 0)],
                                [[bank[b]], [bank[b + 1]]], m == 0, m == 3)
                pe.wait_ge(*conv_u(layer, CT))
                for c, (src, b) in enumerate(((q_sb, 2), (q_sb, 3), (k_sb, 4), (k_sb, 5))):
                    pe.wait_ge(*rotated(layer, 2 if c < 2 else 4))
                    for k in range(2):
                        pair = 2 * (c % 2) + k
                        for t in range(TT):
                            last = nc.tensor.transpose(
                                bank[b][:, k * SEQ + t * P:k * SEQ + (t + 1) * P],
                                src[:, t, pair * P:(pair + 1) * P], ident[:, :])
                    last.then_inc(*qk_ps.one)

                def scores(g):
                    if g >= 2:
                        pe.wait_ge(*sc_used(layer, g - 1))
                    rows = slice(DH * (g % 2), DH * (g % 2) + DH)
                    mm(bank[6 + g % 2][:, 0:P], q_t[rows, g // 2, 0:P], k_t[rows, g // 2, 0:P],
                       start=True, stop=True)
                    mm(bank[6 + g % 2][:, P:3 * P], q_t[rows, g // 2, P:2 * P],
                       k_t[rows, g // 2, :], start=True, stop=True).then_inc(*sc_ps.one)

                def probs_transposed(g):
                    pe.wait_ge(*pr_done(layer, g + 1))
                    if g >= 2:
                        pe.wait_ge(*pt_done(layer, g - 1))
                    for c in range(3):
                        last = nc.tensor.transpose(bank[4 + g % 2][:, c * P:(c + 1) * P],
                                                   pr[:, g, c * P:(c + 1) * P], ident[:, :])
                    last.then_inc(*pt_ps.one)

                def weighted_values(pair):
                    if pair >= 2:
                        pe.wait_ge(*mix_lo(layer, pair - 1))
                    for e in range(2):
                        g = 2 * pair + e
                        pe.wait_ge(*pt_done(layer, g + 1))
                        rows, cols = slice(DH * e, DH * e + DH), slice(g * DH, (g + 1) * DH)
                        dst = bank[pair % 2]
                        mm(dst[rows, 0:SEQ], v_sb[:, 0, cols],
                           p_t[:, g, 0:2 * P], start=True, stop=False)
                        last = mm(dst[rows, P:SEQ], v_sb[:, 1, cols], p_t[:, g, 2 * P:3 * P],
                                  start=False, stop=True)
                    last.then_inc(*pv_ps.one)

                pe.wait_ge(*qk_done(layer, 4))
                scores(0)
                scores(1)
                pe.wait_ge(*acc_done(layer, 1))
                for c in range(CT):
                    last = mm(bank[3][:, 0:SEQ], ones[:, :], acc[:, c, :], start=c == 0,
                              stop=c == CT - 1)
                last.then_inc(*mean_ps.one)
                pe.wait_ge(*v_done(layer, TT))
                for g in range(HEADS):
                    probs_transposed(g)
                    if g + 2 < HEADS:
                        scores(g + 2)
                    if g == 1:
                        pe.wait_ge(*sq_done(layer, 1))
                        for c in range(CT):
                            last = mm(bank[2][:, 0:SEQ], ones[:, :], sq[:, c, :], start=c == 0,
                                      stop=c == CT - 1)
                        last.then_inc(*var_ps.one)
                    if g >= 3 and g % 2:
                        weighted_values(g // 2 - 1)
                weighted_values(PAIRS - 1)
                pe.wait_ge(*mix_lo(layer, PAIRS + 1))
                for n in range(WO0, WQ0):
                    pe.wait_ge(*lo_done(layer, n + 1))
                    by_tile(n % RING, mixed_part, [(n - WO0, 0, 0), (n - WO0, HALF, 1)],
                            model_banks, n == WO0, n == WQ0 - 1)
                pe.wait_ge(*x1_ready(layer, TT))
                transpose_x()
                pe.wait_ge(*xt_lo(layer, 8))
                for n in range(WQ0, U0):
                    pe.wait_ge(*lo_done(layer, n + 1))
                    if n >= WQ0 + 8:
                        pe.wait_ge(*qp_done(layer, n - WQ0 - 7))
                    tile_by_x(n % RING, bank[n % 8][:, 0:SEQ])
                pe.wait_ge(*qp_done(layer, HC))
                pe.wait_ge(*keys_in(layer, 1))
                for t in range(TT):
                    for c in range(4):
                        for k in range(4):
                            g = 4 * c + k
                            last = mm(bank[4 * t + c][:, k * NK:(k + 1) * NK],
                                      qp_t[:, g, t * P:(t + 1) * P], keys_sb[:, g, :],
                                      start=True, stop=True)
                        last.then_inc(*sp_ps.one)

                def u_turn(i, first=False):
                    for j in range(RING):
                        pe.wait_ge(*lo_done(layer, RING * i + (U0 + j + 1)))
                        if not first:
                            pe.wait_ge(*gelu_done(layer, RING * i + (j - RING + 1)))
                        tile_by_x(j, ring_banks[j][:, 0:SEQ])

                pe.wait_ge(*s_done(layer, TT * 4))
                u_turn(0, first=True)
                with pe.Fori(1, T_TURN) as i:
                    u_turn(i)
                pe.wait_ge(*chosen(layer, 1))
                for t in range(TT):
                    for c, src in enumerate((e1, e2, gate)):
                        last = nc.tensor.transpose(
                            bank[t][:, c * P:(c + 1) * P],
                            src[:, t].rearrange("p g k -> p (g k)"), ident[:, :])
                    last.then_inc(*chosen_ps.one)
                with pe.Fori(T_TURN, TURNS) as i:
                    u_turn(i)

                pe.wait_ge(*gelu_done(layer, NK))

                def gate_matrices(i, b, first=False):
                    pe.wait_ge(*gated_done(layer, 2 * i + (b + 1)))
                    if not first:
                        pe.wait_ge(*w_done(layer, 2 * i + (b - 1)))
                    for t in range(GROUP):
                        dst = ring_banks[b][:, t * NK:(t + 1) * NK]
                        mm(dst, one_b[:, b, t, :], a_hi[:, b, t, :], start=True, stop=False)
                        last = mm(dst, one_b[:, b, t, :], a_lo[:, b, t, :], start=False, stop=True)
                    last.then_inc(*g_ps.one)

                for b in range(2):
                    gate_matrices(0, b, first=True)
                with pe.Fori(1, GROUPS // 2) as i:
                    for b in range(2):
                        gate_matrices(i, b)

                def v_turn(i, first=False, final=False):
                    for j in range(RING):
                        pe.wait_ge(*lo_done(layer, RING * i + (V0 + j + 1)))
                        pe.wait_ge(*wlo_done(layer, RING * i + (j + 1)))
                        by_tile(j, lambda part, t, k, j=j: ws[:, j, part, t * P:(t + 1) * P],
                                [(0, 0, 0), (0, HALF, 1)], model_banks,
                                first and j == 0, final and j == RING - 1)

                v_turn(0, first=True)
                with pe.Fori(1, LAST) as i:
                    v_turn(i)
                v_turn(LAST, final=True)


def rope_table():
    inv = np.power(np.float32(10000.0), -np.arange(0, DH, 2, dtype=np.float32) / DH)
    ang = np.arange(SEQ, dtype=np.float32)[:, None] * inv[None, :].astype(np.float32)
    cos, sin = np.cos(ang), np.sin(ang)
    both = np.stack([np.concatenate([cos, cos], 1), np.concatenate([-sin, sin], 1)], 1)
    return both.reshape(TT, P, 2, DH).transpose(1, 0, 2, 3).astype(np.float32)


def causal_table():
    tri = np.where(np.arange(P)[None, :] <= np.arange(P)[:, None], 0.0, MASKED)
    return np.concatenate([tri, np.zeros((P, P)), tri], 1).astype(np.float32)


def kernel(x, w_in, conv_w, conv_b, conv_ln_g, conv_ln_b, w_out, ln1_g, ln1_b,
           peer_wq, peer_keys, peer_u, peer_v, ln2_g, ln2_b):
    import concourse.bacc as bacc
    from concourse.bass_utils import run_bass_kernel_spmd

    w_in, w_out, peer_wq, peer_u, peer_v = map(np.asarray, (w_in, w_out, peer_wq, peer_u, peer_v))
    L = DEPTH
    ag = w_in[:, :, 3 * AW:].reshape(L, KC, P, 2, CT, P).transpose(0, 4, 3, 2, 1, 5)
    qkv = w_in[:, :, :3 * AW].reshape(L, KC // 2, 2, P, 3, AW).transpose(0, 4, 1, 3, 2, 5)
    wq = peer_wq.reshape(L, KC, P, HC, P).transpose(0, 3, 2, 1, 4)
    u = peer_u.reshape(L, NK, NK, KC, P).transpose(0, 1, 4, 3, 2)
    stream = np.concatenate([ag.reshape(L, -1, D), qkv.reshape(L, -1, D), w_out.reshape(L, -1, D),
                             wq.reshape(L, -1, D), u.reshape(L, -1, D),
                             peer_v.reshape(L, -1, D)], axis=1).reshape(-1, D)
    keys_t = np.asarray(peer_keys).transpose(0, 4, 1, 2, 3).reshape(L * P, HC * NK)
    conv_p = np.concatenate([np.asarray(conv_w), np.asarray(conv_b)[:, None],
                             np.asarray(conv_ln_g)[:, None], np.asarray(conv_ln_b)[:, None]], 1)
    conv_p = conv_p.reshape(L, TAPS + 3, CT, P).transpose(0, 3, 2, 1).reshape(L * P, -1)
    ln_p = np.stack([np.asarray(a) for a in (ln1_g, ln1_b, ln2_g, ln2_b)], 1).reshape(L * 4, D)
    arrays = {
        "x": np.asarray(x).reshape(SEQ, D), "stream": stream, "keys_t": keys_t, "conv_p": conv_p,
        "ln_p": ln_p, "rope": rope_table().reshape(P, -1), "causal": causal_table(),
    }
    arrays = {name: np.ascontiguousarray(a) for name, a in arrays.items()}

    nc = bacc.Bacc("TRN2", target_bir_lowering=False, num_devices=1)
    args = [nc.dram_tensor(f"in_{name}", a.shape, mybir.dt.float32, kind="ExternalInput").ap()
            for name, a in arrays.items()]
    result = nc.dram_tensor("result", (SEQ, D), mybir.dt.float32, kind="ExternalOutput").ap()
    build(nc, *args, result)
    r = run_bass_kernel_spmd(nc, [{f"in_{name}": a for name, a in arrays.items()}], core_ids=[0])
    return np.asarray(r.results[0]["result"]).reshape(1, SEQ, D)
```

```python
from contextlib import ExitStack

import numpy as np
import concourse.bass as bass
from concourse import mybir

P = 128
SEQ, D, DEPTH = 256, 1024, 2
HEADS, DH = 8, 64
AW = HEADS * DH
CW = D - AW
TAPS = 31
PH, NK, TOPK = 8, 128, 16
HC = 2 * PH
ALPHA = (2 * DEPTH) ** 0.25
EPS = 1e-5
SCALE = DH ** -0.5
MASKED = -1e30
LOWEST = -3e38

TT = SEQ // P
KC = D // P
CT = CW // P
PAIRS = HEADS // 2
HALF = D // 2

AG0, QKV0 = 0, 2 * CT
WO0 = QKV0 + 3 * (KC // 2)
WQ0 = WO0 + KC
U0 = WQ0 + HC
V0 = U0 + NK
TILES = V0 + NK
RING = 4
HI_LEAD, LO_LEAD = 3, 2
WHI_LEAD, WLO_LEAD = 2, 1
GROUP = 4
GROUPS = SEQ // GROUP
assert GROUPS == NK // 2
PROD_RING = 3
TURNS = NK // RING
LAST = TURNS - 1
TOP_GROUPS = 8
A_TURNS = TT * HC // TOP_GROUPS
PAIR_HEADS = 2
B_TURNS = PH // PAIR_HEADS
C_TURNS = PH // PAIR_HEADS
TOP_TURNS = A_TURNS + B_TURNS + C_TURNS
G_TURN = TURNS // 2
PARTS = 3
SEG = NK // 2
WIDE, NARROW = 4, 4
WIDE_SUMS = WIDE * TOPK
SUMS = WIDE_SUMS + (TOPK - WIDE) * NARROW
assert (WIDE + 1) * (NARROW + 1) > TOPK
DVE_STEPS = 499


class Signal:

    def __init__(self, ctx, nc, name, per_layer, unit=1, primed=0):
        self.sem = ctx.enter_context(nc.semaphore(name))
        self.per_layer, self.unit, self.primed = per_layer, unit, primed
        self.one = (self.sem, unit)

    def __call__(self, layer, k):
        return self.sem, (layer * self.per_layer + k + self.primed) * self.unit


class Steps:

    def __init__(self, engine, sem, base, per_turn):
        self.engine, self.sem, self.per_turn = engine, sem, per_turn
        self.base, self.n = base, 0

    def __call__(self, instruction):
        instruction.then_inc(self.sem, 1)
        self.n += 1
        return self.n

    def settle(self, n=None):
        self.engine.wait_ge(self.sem, self.base + (self.n if n is None else n))

    def settle_alone(self, held):
        self.settle()
        self.engine.sem_inc(held, 1)

    def turn(self, i, per_turn):
        return Steps(self.engine, self.sem, self.base + self.n + i * per_turn, per_turn)

    def ended(self, turn, turns=1):
        assert turn.n == turn.per_turn, (turn.n, turn.per_turn)
        self.n += turns * turn.n


def build(nc, x_in, stream, keys_t, conv_p, ln_p, rope, causal, x1_dram, out):
    f32, f32r, u32, bf16 = (mybir.dt.float32, mybir.dt.float32r, mybir.dt.uint32,
                            mybir.dt.bfloat16)
    ALU, ACT = mybir.AluOpType, mybir.ActivationFunctionType
    X = mybir.AxisListType.X
    ds = bass.ds

    ctx = ExitStack()
    with ctx:
        start = (nc.sbuf_base + 31) // 32 * 32
        used = [start]

        def place(name, shape, dt=f32, at=None):
            size = int(np.prod(shape[1:])) * (2 if dt == bf16 else 4)
            if at is None:
                at = used[0]
                used[0] += size
            return nc.alloc_sbuf_tensor_at(name, shape, dt, offset=at)

        raw = place("raw", [P, RING, D])
        hi = place("hi", [P, RING, D], f32r)
        lo = place("lo", [P, RING, D], f32r)
        x_at = used[0]
        x = place("x", [P, TT, D])
        gated_a = place("gated_a", [P, 2, PARTS, GROUP, SEG], bf16, at=x_at)
        one_b = place("onehot_b", [P, 2, GROUP, NK], bf16, at=x_at + 3072)
        one_a = place("onehot_a", [P, 2, GROUP, SEG], bf16, at=x_at + 5120)
        ident = place("ident", [P, P])
        iota = place("iota", [P, P])
        i1_t = place("i1_t", [P, SEQ])
        i2_t = place("i2_t", [P, SEQ])
        gate_part = place("gate_part", [P, PARTS, SEQ], bf16)
        gate_rest = place("gate_rest", [P, PARTS - 1, P])
        xt_at = used[0]
        xt = place("xt", [P, KC, 2, SEQ], f32r)
        ws = place("w_split", [P, RING, 2, SEQ], f32r, at=xt_at)
        ones = place("ones", [P, P])
        small = place("small", [P, 160])
        act = used[0]
        h = place("h", [P, NK * SEQ])
        assert used[0] <= nc.sbuf_top, used[0]
        h_tok = h[:, :].rearrange("p (b t) -> p t b", t=SEQ)

        def inside(name, at, shape, dt=f32):
            assert at + int(np.prod(shape[1:])) * 4 <= NK * SEQ * 4
            return place(name, shape, dt, at=act + at)

        ln2_g, ln2_b = inside("ln2_g", 0, [P, D]), inside("ln2_b", 4096, [P, D])
        ln1_g, ln1_b = inside("ln1_g", 8192, [P, D]), inside("ln1_b", 12288, [P, D])
        rope_sb = inside("rope_sb", 16384, [P, TT, 2, DH])
        causal_sb = inside("causal_sb", 17408, [P, 3 * P])
        conv_sb = inside("conv_sb", 18944, [P, CT, TAPS + 3])
        u_pad = inside("u_pad", 19968, [P, CT, 288])
        acc = inside("conv_acc", 24576, [P, CT, SEQ])
        xc = inside("conv_centred", 28672, [P, CT, SEQ])
        sq = inside("conv_squares", 32768, [P, CT, SEQ])
        prod = inside("conv_products", 28672, [P, PROD_RING, 2, SEQ])
        sg = inside("sigmoid", 36864, [P, CT, SEQ])
        rstd = inside("conv_rstd", 40960, [P, 2, SEQ])
        q_sb = inside("q_rotated", 43008, [P, TT, AW])
        k_sb = inside("k_rotated", 47104, [P, TT, AW])
        m1, m2 = inside("rope_cos_part", 51200, [P, AW]), inside("rope_sin_part", 53248, [P, AW])
        v_sb = inside("v", 55296, [P, TT, AW])
        q_t = inside("q_t", 59392, [P, PAIRS, SEQ])
        k_t = inside("k_t", 63488, [P, PAIRS, SEQ])
        sm = inside("masked_scores", 67584, [P, HEADS, 3 * P])
        pr = inside("probs", 79872, [P, HEADS, 3 * P])
        p_t = inside("probs_t", 92160, [P, HEADS, 3 * P])
        mixed = inside("mixed", 104448, [P, KC, 2, SEQ], f32r)
        res = inside("residual", 120832, [P, TT, D])
        qp_t = inside("peer_q_t", 19968, [P, HC, SEQ])
        keys_sb = inside("keys_sb", 67584, [P, HC, NK])
        s_at = (NK * 3 // 4) * SEQ * 4
        s_sb = inside("scores", s_at, [P, TT * HC * NK])
        t0 = s_at + TT * HC * NK * 4
        sg_in = inside("topk_in", t0, [P, TOP_GROUPS, NK])
        sg_rest = inside("topk_rest", t0 + 4096, [P, TOP_GROUPS, NK])
        top_v8 = inside("top_values_now", t0 + 8192, [P, TOP_GROUPS, TOPK])
        top_i8 = inside("top_index_now", t0 + 8704, [P, TOP_GROUPS, TOPK], u32)
        top_v = inside("top_values", t0 + 9216, [P, TT, HC, TOPK])
        top_i = inside("top_index", t0 + 11264, [P, TT, HC, TOPK])
        best_v = inside("best_values", t0 + 13312, [P, TT, PH, TOPK])
        best_c = inside("best_places", t0 + 14336, [P, TT, PH, TOPK], u32)
        gate = inside("gates", t0 + 15360, [P, TT, PH, TOPK])
        comb = inside("pair_sums", t0, [P, PAIR_HEADS * TT, SUMS])
        comb_rest = inside("pair_sums_rest", t0 + 4096, [P, PAIR_HEADS * TT, SUMS])
        cmp = inside("place_matches", t0, [P, 2, TT, TOPK, TOPK])
        hit = inside("matched_keys", t0 + 4096, [P, 2, TT, TOPK, TOPK])
        def late(name, n, dt=f32):
            return inside(name, s_at + 1024 * n, [P, TT, PH, TOPK], dt)

        e1, e2, row_u, col_u = late("first_keys", 0), late("second_keys", 1), late("row_place", 2, u32), late("column_place", 3, u32)
        row_f, col_f, narrow_u, narrow_f = late("row_place_f", 4), late("column_place_f", 5), late("narrow_place", 6, u32), late("narrow_place_f", 7)
        is_narrow, place_f = late("is_narrow", 8), late("place_f", 9)
        best_v4 = inside("best_values_now", s_at + 10240, [P, PAIR_HEADS * TT, TOPK])
        best_c4 = inside("best_places_now", s_at + 10496, [P, PAIR_HEADS * TT, TOPK], u32)
        gate_sum = inside("gate_sums", s_at + 10752, [P, TT, PH])
        gate_inv = inside("gate_inverses", s_at + 10816, [P, TT, PH])

        cut = [0]

        def piece(n):
            cut[0] += n
            assert cut[0] <= 160
            return small[:, cut[0] - n:cut[0]]

        row_max, neg_max, row_sum, row_inv = piece(16), piece(16), piece(16), piece(16)
        ln_stats, ln_mv, ln_std, ln_rstd = piece(24), piece(4), piece(2), piece(2)

        bank = [ctx.enter_context(nc.psum_tensor(f"bank{n}", [P, 512], f32)) for n in range(8)]
        acc_banks = bank[0:4]
        ring_banks = bank[4:8]

        def signal(name, per_layer, unit=1, primed=0):
            return Signal(ctx, nc, name, per_layer, unit, primed)

        raw_in = [signal(f"raw_in{j}", TILES // RING, 16) for j in range(RING)]
        hi_done = signal("hi_done", TILES)
        lo_done = [signal(f"lo_done{j}", TILES // RING) for j in range(RING)]
        tile_used = signal("tile_used", TILES, primed=RING)
        x_loaded = signal("x_loaded", 1, 16)
        consts_made = signal("consts_made", 1)
        pool_setup = signal("pool_setup", 1)
        x_ready = signal("x_ready", TT, primed=TT)
        params_in = signal("params_in", 5, 16)
        keys_in = signal("keys_in", 1, 16)
        ln2_in = signal("ln2_params_in", 2, 16)
        xt_ps, xt_hi, xt_lo = signal("xt_ps", 8), signal("xt_hi", 8), signal("xt_lo", 8)
        sig_done, conv_u = signal("sigmoid_done", CT), signal("conv_u", CT)
        rotated, v_done = signal("rotated", 2 * TT), signal("v_done", TT)
        qk_ps, qk_done = signal("qk_t_ps", 4), signal("qk_t_done", 4)
        sc_ps, sc_used = signal("scores_ps", HEADS), signal("scores_masked", HEADS)
        max_done, exp_done = signal("max_done", HEADS), signal("exp_done", 2 * HEADS)
        pr_done, pt_ps = signal("probs_done", HEADS), signal("probs_t_ps", HEADS)
        pt_done, pv_ps = signal("probs_t_done", HEADS), signal("pv_ps", PAIRS)
        mix_hi, mix_lo = signal("mixed_hi", PAIRS), signal("mixed_lo", PAIRS)
        mix_conv_hi, mix_conv = signal("mixed_conv_hi", 1), signal("mixed_conv", 1)
        acc_done, mean_ps = signal("conv_done", 1), signal("conv_mean_ps", 1)
        centred, sq_done = signal("conv_centred_done", 1), signal("conv_squares_done", 1)
        var_ps, var_done = signal("conv_var_ps", 1), signal("conv_var_done", 1)
        std_done, normed = signal("conv_std_done", 1), signal("conv_normed", 1)
        silu_done = signal("silu_done", CT)
        ln_var, ln_root = signal("ln_var", 2 * TT), signal("ln_root", 2 * TT)
        x1_ready = signal("x1_ready", TT)
        x1_kept, x1_back = signal("x1_in_dram", TT, 16), signal("x1_back", TT, 16)
        conv_first, prod_done = signal("conv_first_tap", 1), signal("conv_product", TAPS - 1)
        prod_used = signal("conv_product_added", TAPS - 1)
        qp_done, sp_ps = signal("peer_q_done", HC), signal("peer_scores_ps", TT * 4)
        s_done = signal("peer_scores_done", TT * 4)
        top_in, top_in_used = signal("topk_in_ready", A_TURNS), signal("topk_in_used", A_TURNS)
        best_done, gate_exp = signal("best_done", 1), signal("gate_exp", 1)
        chosen, chosen_ps = signal("chosen", 1), signal("chosen_t_ps", TT)
        tables = signal("chosen_tables", TT)
        gelu_done = signal("gelu_done", NK, primed=RING)
        one_done, gated_done = signal("onehots_done", NK), signal("gated_done", NK)
        g_ps, w_done = signal("gate_matrix_ps", NK), signal("w_done", NK, primed=2)
        whi_done, wlo_done = signal("w_hi_done", NK), signal("w_lo_done", NK)
        out_done = signal("out_done", 1, 16)
        pe_held = ctx.enter_context(nc.semaphore("pe_held"))
        dve_held = ctx.enter_context(nc.semaphore("dve_held"))
        pool_held = ctx.enter_context(nc.semaphore("pool_held"))
        dve_steps = ctx.enter_context(nc.semaphore("dve_steps"))

        block = ctx.enter_context(nc.Block())

        @block.sync
        def _(sp):
            for t in range(TT):
                sp.dma_start(x[:, t, :], x_in[t * P:(t + 1) * P, :]).then_inc(*x_loaded.one)
            for j in range(RING):
                sp.dma_start(raw[:, j, :], stream[j * P:(j + 1) * P, :]).then_inc(*raw_in[j].one)
            with sp.Fori(1, DEPTH * TILES // RING) as turn:
                for j in range(RING):
                    sp.wait_ge(*lo_done[j](0, turn))
                    sp.dma_start(raw[:, j, :], stream[ds((RING * turn + j) * P, P), :])\
                      .then_inc(*raw_in[j].one)
            sp.wait_ge(*x_ready(DEPTH - 1, TT))
            for t in range(TT):
                sp.dma_start(out[t * P:(t + 1) * P, :], x[:, t, :]).then_inc(*out_done.one)
            sp.wait_ge(*out_done(0, TT))

        @block.gpsimd
        def _(pool):
            nc.gpsimd.iota(iota[:, :], pattern=[[1, P]], base=0, channel_multiplier=0,
                           allow_small_or_imprecise_dtypes=True)
            nc.gpsimd.memset(ones[:, :], 1.0 / CW)
            nc.gpsimd.memset(ident[:, :], 0.0).then_inc(*pool_setup.one)
            pool.wait_ge(*pool_setup(0, 1))
            nc.gpsimd.affine_select(out=ident[:, :], in_=ident[:, :], compare_op=ALU.not_equal,
                                    fill=1.0, base=0, pattern=[[-1, P]], channel_multiplier=1)\
              .then_inc(*consts_made.one)
            for _ in range(2):
                pool.sem_inc(w_done.sem, 1)
            with pool.Fori(0, DEPTH) as layer:
                pool.wait_ge(*conv_first(layer, 1))
                pool.sem_inc(pool_held, 1)
                with pool.Fori(0, (TAPS - 1) // PROD_RING) as i:
                    for c in range(PROD_RING):
                        pool.wait_ge(*prod_done(layer, PROD_RING * i + (c + 1)))
                        if c:
                            pool.wait_ge(*prod_used(layer, PROD_RING * i + c))
                        nc.gpsimd.tensor_tensor(acc[:, 2:4, :], acc[:, 2:4, :], prod[:, c, :, :],
                                                ALU.add).then_inc(*prod_used.one)
                    pool.wait_ge(*prod_used(layer, PROD_RING * i + PROD_RING))
                    pool.sem_inc(pool_held, 1)

                def rest(turn, j):
                    pool.wait_ge(*hi_done(layer, RING * turn + (j + 1)))
                    nc.gpsimd.tensor_tensor(lo[:, j, :], raw[:, j, :], hi[:, j, :].bitcast(f32),
                                            ALU.subtract).then_inc(*lo_done[j].one)

                with pool.Fori(U0 // RING, U0 // RING + TOP_TURNS) as turn:
                    rest(turn, 3)
                    rest(turn + 1, 1)

                def gated(seg, i, j):
                    pool.wait_ge(*one_done(layer, seg * GROUPS + RING * i + (j + 1)))
                    tok, b = ds(i * (RING * GROUP) + j * GROUP, GROUP), j % 2
                    for part in range(PARTS):
                        last = nc.gpsimd.tensor_tensor(
                            gated_a[:, b, part], one_a[:, b],
                            gate_part[:, part, tok][:, :, None].to_broadcast([P, GROUP, SEG]),
                            ALU.mult)
                    last.then_inc(*gated_done.one)

                with pool.Fori(0, TURNS - G_TURN) as i:
                    for j in range(RING):
                        gated(0, i, j)

                def w_rest(i, j):
                    i, j = i + j // RING, j % RING
                    pool.wait_ge(*whi_done(layer, RING * i + (j + 1)))
                    nc.gpsimd.tensor_tensor(
                        ws[:, j, 1, :], h[:, ds(i * (RING * SEQ) + j * SEQ, SEQ)],
                        ws[:, j, 0, :].bitcast(f32), ALU.subtract).then_inc(*wlo_done.one)

                w_rest(0, 0)
                with pool.Fori(0, G_TURN) as i:
                    for j in range(RING):
                        gated(1, i, j)
                        w_rest(i, j + 1)
                with pool.Fori(G_TURN, LAST) as i:
                    for j in range(RING):
                        w_rest(i, j + 1)
                for j in range(RING - 1):
                    w_rest(LAST, j + 1)

        @block.scalar
        def _(act):
            act.wait_ge(*consts_made(0, 1))
            for _ in range(RING):
                act.sem_inc(gelu_done.sem, 1)
            with act.Fori(0, DEPTH) as layer:

                def head(turn, j):
                    turn, j = turn + j // RING, j % RING
                    act.wait_ge(*raw_in[j](layer, turn + 1))
                    act.wait_ge(*tile_used(layer, RING * turn + (j - RING + 1)))
                    nc.scalar.activation(hi[:, j, :], raw[:, j, :], ACT.Copy).then_inc(*hi_done.one)

                def x_heads(done):
                    for c in range(4):
                        act.wait_ge(*xt_ps(layer, done + c + 1))
                        nc.scalar.activation(
                            xt[:, 2 * c:2 * c + 2, 0, :],
                            ring_banks[c][:, :].rearrange("p (k t) -> p k t", k=2), ACT.Copy)\
                          .then_inc(*xt_hi.one)

                act.wait_ge(*x_ready(layer, 0))
                act.dma_start(conv_sb[:, :, :], conv_p[ds(layer * P, P), :])\
                   .then_inc(*params_in.one)
                act.dma_start(rope_sb[:, :, :, :], rope).then_inc(*params_in.one)
                act.dma_start(causal_sb[:, :], causal).then_inc(*params_in.one)
                act.dma_start(ln1_g[:, :], ln_p[ds(layer * 4, 1), :].to_broadcast([P, D]))\
                   .then_inc(*params_in.one)
                act.dma_start(ln1_b[:, :], ln_p[ds(layer * 4 + 1, 1), :].to_broadcast([P, D]))\
                   .then_inc(*params_in.one)
                for n in range(HI_LEAD):
                    head(0, n)
                x_heads(0)
                for n in range(AG0, QKV0):
                    head(0, n + HI_LEAD)
                    if n % 2:
                        act.wait_ge(*tile_used(layer, n + 1))
                        nc.scalar.activation(sg[:, n // 2, :], bank[(4 + n) % 8][:, 0:SEQ],
                                             ACT.Sigmoid).then_inc(*sig_done.one)

                def conv_products(first, last):
                    for tap in range(first, last):
                        if tap > PROD_RING:
                            act.wait_ge(*prod_used(layer, tap - PROD_RING))
                        for c in range(2):
                            window = u_pad[:, 2 + c, tap:tap + SEQ]
                            weight = conv_sb[:, 2 + c, tap:tap + 1]
                            if tap == 0:
                                end = nc.scalar.activation(
                                    acc[:, 2 + c, :], window, ACT.Identity, scale=weight,
                                    bias=conv_sb[:, 2 + c, TAPS:TAPS + 1])
                            else:
                                end = nc.scalar.activation(prod[:, (tap - 1) % PROD_RING, c, :],
                                                           window, ACT.Copy, scale=weight)
                        end.then_inc(*(conv_first if tap == 0 else prod_done).one)

                act.wait_ge(*params_in(layer, 5))
                act.wait_ge(*conv_u(layer, CT))
                n_qkv = WO0 - QKV0
                for n in range(n_qkv):
                    head(0, QKV0 + n + HI_LEAD)
                    conv_products(TAPS * n // n_qkv, TAPS * (n + 1) // n_qkv)
                act.wait_ge(*tile_used(layer, WO0))
                for t in range(TT):
                    nc.scalar.activation(v_sb[:, t, :], bank[t][:, :], ACT.Copy)\
                      .then_inc(*v_done.one)
                for c, (dst, b) in enumerate(((q_t, 2), (q_t, 3), (k_t, 4), (k_t, 5))):
                    act.wait_ge(*qk_ps(layer, c + 1))
                    nc.scalar.activation(dst[:, 2 * (c % 2):2 * (c % 2) + 2, :],
                                         bank[b][:, :].rearrange("p (k t) -> p k t", k=2),
                                         ACT.Copy).then_inc(*qk_done.one)

                def probs_transposed(g):
                    act.wait_ge(*pt_ps(layer, g + 1))
                    nc.scalar.activation(p_t[:, g, :], bank[4][:, 0:3 * P], ACT.Copy)\
                      .then_inc(*pt_done.one)

                def pv_heads(pair):
                    act.wait_ge(*pv_ps(layer, pair + 1))
                    nc.scalar.activation(mixed[:, pair, 0, :],
                                         bank[5][:, 0:SEQ],
                                         ACT.Copy).then_inc(*mix_hi.one)

                for g in range(HEADS):
                    act.wait_ge(*max_done(layer, g + 1))
                    for t, (c0, c1) in enumerate(((0, P), (P, 3 * P))):
                        nc.scalar.activation(pr[:, g, c0:c1], sm[:, g, c0:c1], ACT.Exp,
                                             bias=neg_max[:, 2 * g + t:2 * g + t + 1], scale=SCALE,
                                             accum_out=row_sum[:, 2 * g + t:2 * g + t + 1])\
                          .then_inc(*exp_done.one)
                    if g >= 1:
                        probs_transposed(g - 1)
                    if g == 0:
                        act.wait_ge(*centred(layer, 1))
                        nc.scalar.activation(sq[:, :, :], xc[:, :, :], ACT.Square)\
                          .then_inc(*sq_done.one)
                    if g == 3:
                        act.wait_ge(*var_done(layer, 1))
                        nc.scalar.activation(rstd[:, 0, :], rstd[:, 1, :], ACT.Sqrt)\
                          .then_inc(*std_done.one)
                    if g == 4:
                        act.wait_ge(*normed(layer, 1))
                        for c in range(CT):
                            nc.scalar.activation(sq[:, c, :], xc[:, c, :], ACT.Silu,
                                                 bias=conv_sb[:, c, TAPS + 2:TAPS + 3],
                                                 scale=conv_sb[:, c, TAPS + 1:TAPS + 2])\
                              .then_inc(*silu_done.one)
                        act.wait_ge(*silu_done(layer, CT))
                        nc.scalar.activation(mixed[:, PAIRS:KC, 0, :], sq[:, :, :], ACT.Copy)\
                          .then_inc(*mix_conv_hi.one)
                    if g >= 3 and g % 2:
                        pv_heads(g // 2 - 1)
                    if g >= 5:
                        head(0, WO0 + g - 5 + HI_LEAD)
                probs_transposed(HEADS - 1)
                act.wait_ge(*pt_ps(layer, HEADS))
                act.dma_start(keys_sb[:, :, :], keys_t[ds(layer * P, P), :]).then_inc(*keys_in.one)
                head(0, WO0 + 3 + HI_LEAD)
                pv_heads(PAIRS - 1)
                for n in range(WO0 + 4, WQ0):
                    head(0, n + HI_LEAD)
                for t in range(TT):
                    act.wait_ge(*ln_var(layer, t + 1))
                    nc.scalar.activation(ln_std[:, t:t + 1], ln_mv[:, 2 * t + 1:2 * t + 2], ACT.Sqrt)\
                      .then_inc(*ln_root.one)
                x_heads(4)
                act.wait_ge(*x1_ready(layer, TT))
                for t in range(TT):
                    act.dma_start(x1_dram[t * P:(t + 1) * P, :], x[:, t, :]).then_inc(*x1_kept.one)
                for n in range(WQ0, U0):
                    head(0, n + HI_LEAD)
                    act.wait_ge(*tile_used(layer, n + 1))
                    nc.scalar.activation(qp_t[:, n - WQ0, :], bank[n % 8][:, 0:SEQ], ACT.Copy)\
                      .then_inc(*qp_done.one)
                for c in range(TT * 4):
                    act.wait_ge(*sp_ps(layer, c + 1))
                    nc.scalar.activation(s_sb[:, c * 512:(c + 1) * 512], bank[c][:, :], ACT.Copy)\
                      .then_inc(*s_done.one)

                nc.scalar.preload_act_table(ACT.Gelu)

                def u_turn(i):
                    for j in range(RING):
                        head(i + U0 // RING, j + HI_LEAD)
                        act.wait_ge(*tile_used(layer, RING * i + (U0 + j + 1)))
                        nc.scalar.activation(h[:, ds(i * (RING * SEQ) + j * SEQ, SEQ)],
                                             ring_banks[j][:, 0:SEQ], ACT.Gelu)\
                          .then_inc(*gelu_done.one)

                def stage(i):
                    size = TOP_GROUPS * NK
                    nc.scalar.activation(sg_in[:, :, :].rearrange("p g k -> p (g k)"),
                                         s_sb[:, ds(i * size, size)], ACT.Copy)\
                      .then_inc(*top_in.one)

                act.wait_ge(*s_done(layer, TT * 4))
                stage(0)
                with act.Fori(0, A_TURNS - 1) as i:
                    u_turn(i)
                    act.wait_ge(*top_in_used(layer, i + 1))
                    stage(i + 1)
                with act.Fori(A_TURNS - 1, A_TURNS + B_TURNS) as i:
                    u_turn(i)
                act.wait_ge(*best_done(layer, 1))
                nc.scalar.activation(gate[:, :, :, :], gate[:, :, :, :], ACT.Exp)\
                  .then_inc(*gate_exp.one)
                nc.scalar.preload_act_table(ACT.Gelu)
                with act.Fori(A_TURNS + B_TURNS, G_TURN) as i:
                    u_turn(i)
                act.wait_ge(*tables(layer, TT))
                with act.Fori(G_TURN, TURNS) as i:
                    u_turn(i)

                def w_head(i, j):
                    i, j = i + j // RING, j % RING
                    act.wait_ge(*tile_used(layer, RING * i + (V0 + j - RING + 1)))
                    nc.scalar.activation(ws[:, j, 0, :], h[:, ds(i * (RING * SEQ) + j * SEQ, SEQ)],
                                         ACT.Copy).then_inc(*whi_done.one)

                def v_turn(i):
                    for j in range(RING):
                        head(i + V0 // RING, j + HI_LEAD)
                        w_head(i, j + WHI_LEAD)

                act.wait_ge(*w_done(layer, GROUPS))
                for b in range(WHI_LEAD):
                    w_head(0, b)
                with act.Fori(0, G_TURN - 1) as i:
                    v_turn(i)
                for j in range(RING):
                    head(G_TURN - 1 + V0 // RING, j + HI_LEAD)
                    if j + WHI_LEAD == RING:
                        act.wait_ge(*w_done(layer, NK))
                    w_head(G_TURN - 1, j + WHI_LEAD)
                act.wait_ge(*x1_kept(layer, TT))
                for t in range(TT):
                    act.dma_start(x[:, t, :], x1_dram[t * P:(t + 1) * P, :]).then_inc(*x1_back.one)
                act.wait_ge(*wlo_done(layer, SEG))
                act.dma_start(ln2_g[:, :], ln_p[ds(layer * 4 + 2, 1), :].to_broadcast([P, D]))\
                   .then_inc(*ln2_in.one)
                act.dma_start(ln2_b[:, :], ln_p[ds(layer * 4 + 3, 1), :].to_broadcast([P, D]))\
                   .then_inc(*ln2_in.one)
                with act.Fori(G_TURN, LAST) as i:
                    v_turn(i)
                for j in range(RING):
                    if j + HI_LEAD < RING:
                        head(LAST + V0 // RING, j + HI_LEAD)
                    if j + WHI_LEAD < RING:
                        w_head(LAST, j + WHI_LEAD)
                for t in range(TT):
                    act.wait_ge(*ln_var(layer, TT + t + 1))
                    nc.scalar.activation(ln_std[:, t:t + 1], ln_mv[:, 2 * t + 1:2 * t + 2], ACT.Sqrt)\
                      .then_inc(*ln_root.one)

        @block.vector
        def _(dve):
            vec = nc.vector
            dve.wait_ge(*x_loaded(0, TT))
            dve.wait_ge(*consts_made(0, 1))
            for t in range(TT):
                dve.sem_inc(*x_ready.one)
            with dve.Fori(0, DEPTH) as layer:
                step = Steps(dve, dve_steps, layer * DVE_STEPS, DVE_STEPS)

                def rest(turn, j):
                    turn, j = turn + j // RING, j % RING
                    dve.wait_ge(*hi_done(layer, RING * turn + (j + 1)))
                    vec.tensor_tensor(lo[:, j, :], raw[:, j, :], hi[:, j, :].bitcast(f32),
                                      ALU.subtract).then_inc(*lo_done[j].one)

                def x_rests(done):
                    for c in range(4):
                        dve.wait_ge(*xt_hi(layer, done + c + 1))
                        vec.tensor_tensor(xt[:, 2 * c:2 * c + 2, 1, :],
                                          ring_banks[c][:, :].rearrange("p (k t) -> p k t", k=2),
                                          xt[:, 2 * c:2 * c + 2, 0, :].bitcast(f32),
                                          ALU.subtract).then_inc(*xt_lo.one)

                def layer_norm(which, t, gain, shift, last):
                    for c in range(2):
                        step(vec.scalar_tensor_tensor(
                            res[:, t, c * HALF:(c + 1) * HALF], x[:, t, c * HALF:(c + 1) * HALF],
                            ALPHA, acc_banks[2 * t + c][:, :], ALU.mult, ALU.add))
                    step.settle()
                    for c in range(2):
                        step(vec.bn_stats(ln_stats[:, 12 * t + 6 * c:12 * t + 6 * c + 6],
                                          res[:, t, c * HALF:(c + 1) * HALF]))
                    step.settle_alone(dve_held)
                    mean, var = ln_mv[:, 2 * t:2 * t + 1], ln_mv[:, 2 * t + 1:2 * t + 2]
                    step(vec.bn_aggr(ln_mv[:, 2 * t:2 * t + 2], ln_stats[:, 12 * t:12 * t + 12]))
                    step.settle()
                    vec.tensor_scalar_add(var, var, EPS).then_inc(*ln_var.one)
                    dve.wait_ge(*ln_root(layer, TT * which + t + 1))
                    step(vec.reciprocal(ln_rstd[:, t:t + 1], ln_std[:, t:t + 1]))
                    step.settle()
                    step(vec.tensor_scalar(res[:, t, :], res[:, t, :], mean, ln_rstd[:, t:t + 1],
                                           ALU.subtract, ALU.mult))
                    step.settle()
                    step(vec.tensor_tensor(res[:, t, :], res[:, t, :], gain[:, :], ALU.mult))
                    step.settle()
                    vec.tensor_tensor(x[:, t, :], res[:, t, :], shift[:, :], ALU.add)\
                       .then_inc(*last.one)

                for n in range(LO_LEAD):
                    rest(0, n)
                step(vec.memset(u_pad[:, :, 0:TAPS - 1], 0.0))
                x_rests(0)
                for n in range(AG0, QKV0):
                    rest(0, n + LO_LEAD)
                    if n % 2:
                        dve.wait_ge(*sig_done(layer, n // 2 + 1))
                        vec.tensor_tensor(u_pad[:, n // 2, TAPS - 1:TAPS - 1 + SEQ],
                                          bank[(3 + n) % 8][:, 0:SEQ], sg[:, n // 2, :],
                                          ALU.mult).then_inc(*conv_u.one)
                dve.wait_ge(*conv_u(layer, CT))
                dve.wait_ge(*params_in(layer, 5))

                def taps(first, last):
                    for tap in range(first, last):
                        for c in range(2):
                            window = u_pad[:, c, tap:tap + SEQ]
                            weight = conv_sb[:, c, tap:tap + 1]
                            if tap == 0:
                                step(vec.tensor_scalar(acc[:, c, :], window, weight,
                                                       conv_sb[:, c, TAPS:TAPS + 1],
                                                       ALU.mult, ALU.add))
                            else:
                                step.settle(step.n - 1)
                                step(vec.scalar_tensor_tensor(acc[:, c, :], window, weight,
                                                              acc[:, c, :], ALU.mult, ALU.add))

                def rotate(banks, dst, before):
                    for t in range(TT):
                        if before + t:
                            dve.wait_ge(*rotated(layer, before + t))
                        src = banks[t][:, :].rearrange("p (h a d) -> p h a d", a=2, d=DH // 2)
                        cos = rope_sb[:, t, 0, :][:, None, :].to_broadcast([P, HEADS, DH])
                        sin = rope_sb[:, t, 1, :].rearrange("p (a d) -> p a d", a=2)
                        m2v = m2[:, :].rearrange("p (h a d) -> p h a d", a=2, d=DH // 2)
                        step(vec.tensor_tensor(m1[:, :].rearrange("p (h d) -> p h d", d=DH),
                                               banks[t][:, :].rearrange("p (h d) -> p h d", d=DH),
                                               cos, ALU.mult))
                        for a in range(2):
                            step(vec.tensor_tensor(
                                m2v[:, :, a, :], src[:, :, 1 - a, :],
                                sin[:, a, :][:, None, :].to_broadcast([P, HEADS, DH // 2]),
                                ALU.mult))
                        step.settle()
                        vec.tensor_tensor(dst[:, t, :], m1[:, :], m2[:, :], ALU.add)\
                           .then_inc(*rotated.one)

                n_qkv = WO0 - QKV0
                for n in range(n_qkv):
                    rest(0, QKV0 + n + LO_LEAD)
                    taps(TAPS * n // n_qkv, TAPS * (n + 1) // n_qkv)
                    if n == 5:
                        dve.wait_ge(*tile_used(layer, QKV0 + 4))
                        rotate(bank[4:6], q_sb, 0)
                    if n == 9:
                        dve.wait_ge(*tile_used(layer, QKV0 + 8))
                        rotate(bank[6:8], k_sb, TT)
                step.settle()
                dve.sem_inc(*acc_done.one)

                def mask_and_max(g):
                    dve.wait_ge(*sc_ps(layer, g + 1))
                    vec.tensor_tensor(sm[:, g, :], bank[6 + g % 2][:, 0:3 * P], causal_sb[:, :],
                                      ALU.add).then_inc(*sc_used.one)
                    dve.wait_ge(*sc_used(layer, g + 1))
                    for t, (c0, c1) in enumerate(((0, P), (P, 3 * P))):
                        step(vec.reduce_max(row_max[:, 2 * g + t:2 * g + t + 1], sm[:, g, c0:c1], X))
                    step.settle()
                    vec.tensor_scalar(neg_max[:, 2 * g:2 * g + 2], row_max[:, 2 * g:2 * g + 2],
                                      -SCALE, None, ALU.mult).then_inc(*max_done.one)

                def normalise(g):
                    dve.wait_ge(*exp_done(layer, 2 * g + 2))
                    step(vec.reciprocal(row_inv[:, 2 * g:2 * g + 2], row_sum[:, 2 * g:2 * g + 2]))
                    step.settle()
                    step(vec.tensor_scalar(pr[:, g, 0:P], pr[:, g, 0:P],
                                           row_inv[:, 2 * g:2 * g + 1], None, ALU.mult))
                    vec.tensor_scalar(pr[:, g, P:3 * P], pr[:, g, P:3 * P],
                                      row_inv[:, 2 * g + 1:2 * g + 2], None, ALU.mult)\
                       .then_inc(*pr_done.one)

                def pv_rests(pair):
                    dve.wait_ge(*mix_hi(layer, pair + 1))
                    vec.tensor_tensor(mixed[:, pair, 1, :],
                                      bank[5][:, 0:SEQ],
                                      mixed[:, pair, 0, :].bitcast(f32), ALU.subtract)\
                       .then_inc(*mix_lo.one)

                mask_and_max(0)
                mask_and_max(1)
                dve.wait_ge(*mean_ps(layer, 1))
                vec.tensor_tensor(xc[:, :, :], acc[:, :, :],
                                  bank[3][:, None, 0:SEQ].to_broadcast([P, CT, SEQ]),
                                  ALU.subtract).then_inc(*centred.one)
                for g in range(HEADS):
                    normalise(g)
                    if g + 2 < HEADS:
                        mask_and_max(g + 2)
                    if g == 2:
                        dve.wait_ge(*var_ps(layer, 1))
                        vec.tensor_scalar(rstd[:, 1, :], bank[2][:, 0:SEQ], EPS, None, ALU.add)\
                           .then_inc(*var_done.one)
                    if g == 3:
                        dve.wait_ge(*std_done(layer, 1))
                        step(vec.reciprocal(rstd[:, 1, :], rstd[:, 0, :]))
                        step.settle()
                        vec.tensor_tensor(xc[:, :, :], xc[:, :, :],
                                          rstd[:, 1:2, :].to_broadcast([P, CT, SEQ]), ALU.mult)\
                           .then_inc(*normed.one)
                    if g == 5:
                        dve.wait_ge(*mix_conv_hi(layer, 1))
                        vec.tensor_tensor(mixed[:, PAIRS:KC, 1, :], sq[:, :, :],
                                          mixed[:, PAIRS:KC, 0, :].bitcast(f32), ALU.subtract)\
                           .then_inc(*mix_conv.one)
                    if g >= 3 and g % 2:
                        pv_rests(g // 2 - 1)
                    if g >= 5:
                        rest(0, WO0 + g - 5 + LO_LEAD)
                rest(0, WO0 + 3 + LO_LEAD)
                pv_rests(PAIRS - 1)

                for n in range(WO0 + 4, WQ0):
                    rest(0, n + LO_LEAD)
                dve.wait_ge(*tile_used(layer, WQ0))
                for t in range(TT):
                    layer_norm(0, t, ln1_g, ln1_b, x1_ready)
                x_rests(4)
                for n in range(WQ0, U0):
                    rest(0, n + LO_LEAD)

                def u_rests(i, pool_helps=False):
                    for j in range(0, RING, 2 if pool_helps else 1):
                        rest(i + U0 // RING, j + LO_LEAD)

                def top16(values, index, src, spare, m, now):
                    for r in range(2):
                        this = src if r == 0 else spare
                        low = slice(8 * r, 8 * r + 8)
                        for g in range(m):
                            now(vec.max(values[:, g, low], this[:, g, :]))
                        now.settle_alone(dve_held)
                        for g in range(m):
                            if r == 0:
                                now(vec.match_replace(spare[:, g, :], values[:, g, low],
                                                      this[:, g, :], LOWEST))
                            now(vec.max_index(index[:, g, low], values[:, g, low], this[:, g, :]))
                        now.settle_alone(dve_held)
                        if r == 0 and m == TOP_GROUPS:
                            dve.sem_inc(*top_in_used.one)

                A_STEPS = 5 * TOP_GROUPS + 2
                now_size = TOP_GROUPS * TOPK
                with dve.Fori(0, A_TURNS) as i:
                    now = step.turn(i, A_STEPS)
                    u_rests(i, True)
                    dve.wait_ge(*top_in(layer, i + 1))
                    dve.sem_inc(dve_held, 1)
                    top16(top_v8, top_i8, sg_in, sg_rest, TOP_GROUPS, now)
                    for dst, src in ((top_v, top_v8), (top_i, top_i8)):
                        now(vec.tensor_copy(
                            dst[:, :, :, :].rearrange("p t g k -> p (t g k)")[
                                :, ds(i * now_size, now_size)],
                            src[:, :, :].rearrange("p g k -> p (g k)")))
                    now.settle_alone(dve_held)
                step.ended(now, A_TURNS)

                n_sums = PAIR_HEADS * TT
                B_STEPS = 5 * n_sums + 4 * PAIR_HEADS
                top_v_flat = top_v[:, :, :, :].rearrange("p t g k -> p t (g k)")
                best_v_flat = best_v[:, :, :, :].rearrange("p t g k -> p t (g k)")
                best_c_flat = best_c[:, :, :, :].rearrange("p t g k -> p t (g k)")
                with dve.Fori(0, B_TURNS) as i:
                    now = step.turn(i, B_STEPS)
                    u_rests(i + A_TURNS, True)
                    for e in range(PAIR_HEADS):
                        at = i * (2 * TOPK * PAIR_HEADS) + 2 * TOPK * e
                        sums = comb[:, TT * e:TT * e + TT, :]
                        for cols, a0, n_a, n_b in ((slice(0, WIDE_SUMS), 0, WIDE, TOPK),
                                                   (slice(WIDE_SUMS, SUMS), WIDE, TOPK - WIDE,
                                                    NARROW)):
                            first = top_v_flat[:, :, ds(at + a0, n_a)]
                            second = top_v_flat[:, :, ds(at + TOPK, n_b)]
                            shape = [P, TT, n_a, n_b]
                            now(vec.tensor_tensor(
                                sums[:, :, cols].rearrange("p t (a b) -> p t a b", b=n_b),
                                first[:, :, :, None].to_broadcast(shape),
                                second[:, :, None, :].to_broadcast(shape), ALU.add))
                    now.settle_alone(dve_held)
                    top16(best_v4, best_c4, comb, comb_rest, n_sums, now)
                    for e in range(PAIR_HEADS):
                        at = ds(i * (TOPK * PAIR_HEADS) + TOPK * e, TOPK)
                        now(vec.tensor_copy(best_v_flat[:, :, at],
                                            best_v4[:, TT * e:TT * e + TT, :]))
                        now(vec.tensor_copy(best_c_flat[:, :, at],
                                            best_c4[:, TT * e:TT * e + TT, :]))
                    now.settle_alone(dve_held)
                step.ended(now, B_TURNS)
                vec.tensor_tensor(gate[:, :, :, :].rearrange("p t g k -> p (t g) k"),
                                  best_v[:, :, :, :].rearrange("p t g k -> p (t g) k"),
                                  best_v[:, :, :, 0:1].rearrange("p t g k -> p (t g) k")
                                  .to_broadcast([P, TT * PH, TOPK]),
                                  ALU.subtract).then_inc(*best_done.one)

                def whole(t):
                    return t[:, :, :, :]

                shift, mask = ALU.logical_shift_right, ALU.bitwise_and
                step(vec.tensor_scalar(whole(row_u), whole(best_c), 4, None, shift))
                step(vec.tensor_scalar(whole(col_u), whole(best_c), 15, None, mask))
                step(vec.tensor_scalar(whole(narrow_u), whole(best_c), 2, None, shift))
                step(vec.tensor_copy(whole(place_f), whole(best_c)))
                step.settle()
                step(vec.tensor_copy(whole(row_f), whole(row_u)))
                step(vec.tensor_copy(whole(col_f), whole(col_u)))
                step(vec.tensor_copy(whole(narrow_f), whole(narrow_u)))
                step(vec.tensor_scalar(whole(is_narrow), whole(place_f), float(WIDE_SUMS), None,
                                       ALU.is_ge))
                step.settle()
                step(vec.tensor_scalar(whole(place_f), whole(narrow_f),
                                       float(WIDE - WIDE_SUMS // NARROW), None, ALU.add))
                step(vec.tensor_scalar(whole(narrow_u), whole(best_c), NARROW - 1, None, mask))
                step.settle()
                step(vec.tensor_copy(whole(narrow_f), whole(narrow_u)))
                step(vec.tensor_tensor(whole(place_f), whole(place_f), whole(row_f), ALU.subtract))
                step.settle()
                step(vec.tensor_tensor(whole(narrow_f), whole(narrow_f), whole(col_f),
                                       ALU.subtract))
                step(vec.tensor_tensor(whole(place_f), whole(place_f), whole(is_narrow), ALU.mult))
                step.settle()
                step(vec.tensor_tensor(whole(narrow_f), whole(narrow_f), whole(is_narrow),
                                       ALU.mult))
                step(vec.tensor_tensor(whole(row_f), whole(row_f), whole(place_f), ALU.add))
                step.settle()
                step(vec.tensor_tensor(whole(col_f), whole(col_f), whole(narrow_f), ALU.add))
                step.settle_alone(dve_held)

                C_STEPS = 6 * PAIR_HEADS
                top_i_flat = top_i[:, :, :, :].rearrange("p t g k -> p t (g k)")
                number = iota[:, 0:TOPK][:, None, None, :].to_broadcast([P, TT, TOPK, TOPK])
                with dve.Fori(0, C_TURNS) as i:
                    now = step.turn(i, C_STEPS)
                    u_rests(i + A_TURNS + B_TURNS, True)
                    for e in range(PAIR_HEADS):
                        at = ds(i * (TOPK * PAIR_HEADS) + TOPK * e, TOPK)
                        if e:
                            now.settle()
                        for half, place in enumerate((row_f, col_f)):
                            here = place[:, :, :, :].rearrange("p t g k -> p t (g k)")[:, :, at]
                            now(vec.tensor_tensor(
                                cmp[:, half], here[:, :, :, None].to_broadcast(
                                    [P, TT, TOPK, TOPK]), number, ALU.is_equal))
                        for half in range(2):
                            keys = top_i_flat[:, :, ds(i * (2 * TOPK * PAIR_HEADS)
                                                       + (2 * e + half) * TOPK, TOPK)]
                            now.settle(now.n - 1)
                            now(vec.tensor_tensor(
                                hit[:, half], cmp[:, half],
                                keys[:, :, None, :].to_broadcast([P, TT, TOPK, TOPK]), ALU.mult))
                        for half, dst in enumerate((e1, e2)):
                            now.settle(now.n - 1)
                            now(vec.tensor_reduce(
                                dst[:, :, :, :].rearrange("p t g k -> p t (g k)")[:, :, at],
                                hit[:, half], X, ALU.add))
                    now.settle_alone(dve_held)
                step.ended(now, C_TURNS)
                dve.wait_ge(*gate_exp(layer, 1))
                step(vec.tensor_reduce(gate_sum[:, :, :].rearrange("p t g -> p (t g)"),
                                       gate[:, :, :, :].rearrange("p t g k -> p (t g) k"), X,
                                       ALU.add))
                step.settle()
                step(vec.reciprocal(gate_inv[:, :, :], gate_sum[:, :, :]))
                step.settle()
                vec.tensor_tensor(gate[:, :, :, :].rearrange("p t g k -> p (t g) k"),
                                  gate[:, :, :, :].rearrange("p t g k -> p (t g) k"),
                                  gate_inv[:, :, :].rearrange("p t g -> p (t g)")[:, :, None]
                                  .to_broadcast([P, TT * PH, TOPK]), ALU.mult)\
                   .then_inc(*chosen.one)
                u_rests(TOP_TURNS)
                for t in range(TT):
                    tok = slice(t * P, (t + 1) * P)
                    dve.wait_ge(*chosen_ps(layer, t + 1))
                    step(vec.tensor_copy(i1_t[:, tok], bank[t][:, 0:P]))
                    step(vec.tensor_copy(i2_t[:, tok], bank[t][:, P:2 * P]))
                    left = bank[t][:, 2 * P:3 * P]
                    for part in range(PARTS - 1):
                        step(vec.tensor_copy(gate_part[:, part, tok], left))
                        step.settle()
                        step(vec.tensor_tensor(gate_rest[:, part, :], left,
                                               gate_part[:, part, tok], ALU.subtract))
                        step.settle()
                        left = gate_rest[:, part, :]
                    vec.tensor_copy(gate_part[:, PARTS - 1, tok], left).then_inc(*tables.one)
                    if t + 1 < TT:
                        dve.wait_ge(*tables(layer, t + 1))
                dve.wait_ge(*tables(layer, TT))
                dve.sem_inc(dve_held, 1)
                with dve.Fori(TOP_TURNS + 1, G_TURN) as i:
                    u_rests(i)

                def one_hots(seg, i, j):
                    i, j = i + j // RING, j % RING
                    tok, b = ds(i * (RING * GROUP) + j * GROUP, GROUP), j % 2
                    for dst, src, k0, n in ((one_a, i1_t, seg * SEG, SEG), (one_b, i2_t, 0, NK)):
                        last = vec.tensor_tensor(
                            dst[:, b], iota[:, k0:k0 + n][:, None, :].to_broadcast([P, GROUP, n]),
                            src[:, tok][:, :, None].to_broadcast([P, GROUP, n]), ALU.is_equal)
                    last.then_inc(*one_done.one)

                def gate_block(seg, i, j):
                    dve.wait_ge(*g_ps(layer, seg * GROUPS + RING * i + (j + 1)))
                    here = h_tok[:, ds(i * (RING * GROUP) + j * GROUP, GROUP),
                                 seg * SEG:(seg + 1) * SEG]
                    src = (acc_banks, ring_banks)[seg][j % 2][:, 0:GROUP * SEG]
                    vec.tensor_tensor(here, src.rearrange("p (t b) -> p t b", b=SEG), here,
                                      ALU.mult).then_inc(*w_done.one)

                dve.wait_ge(*x1_kept(layer, TT))
                one_hots(0, 0, 0)
                dve.wait_ge(*gelu_done(layer, SEG))
                dve.sem_inc(dve_held, 1)
                with dve.Fori(0, TURNS - G_TURN - 1) as i:
                    for j in range(RING):
                        one_hots(0, i, j + 1)
                        rest(i + G_TURN + U0 // RING, j + LO_LEAD)
                        gate_block(0, i, j)
                for j in range(RING):
                    if j + 1 < RING:
                        one_hots(0, TURNS - G_TURN - 1, j + 1)
                    else:
                        one_hots(1, 0, 0)
                    rest(LAST + U0 // RING, j + LO_LEAD)
                    gate_block(0, TURNS - G_TURN - 1, j)

                dve.wait_ge(*gelu_done(layer, NK))
                dve.sem_inc(dve_held, 1)
                with dve.Fori(0, G_TURN - 1) as i:
                    for j in range(RING):
                        one_hots(1, i, j + 1)
                        rest(i + V0 // RING, j + LO_LEAD)
                        gate_block(1, i, j)
                for j in range(RING):
                    if j + 1 < RING:
                        one_hots(1, G_TURN - 1, j + 1)
                    rest(G_TURN - 1 + V0 // RING, j + LO_LEAD)
                    gate_block(1, G_TURN - 1, j)
                with dve.Fori(G_TURN, LAST) as i:
                    for j in range(RING):
                        rest(i + V0 // RING, j + LO_LEAD)
                for j in range(RING - LO_LEAD):
                    rest(LAST + V0 // RING, j + LO_LEAD)
                dve.wait_ge(*x1_back(layer, TT))
                dve.wait_ge(*tile_used(layer, TILES))
                dve.wait_ge(*ln2_in(layer, 2))
                for t in range(TT):
                    layer_norm(1, t, ln2_g, ln2_b, x_ready)
                assert step.n == DVE_STEPS, step.n

        @block.tensor
        def _(pe):
            mm = nc.tensor.matmul
            for _ in range(RING):
                pe.sem_inc(tile_used.sem, 1)
            pe.wait_ge(*consts_made(0, 1))
            with pe.Fori(0, DEPTH) as layer:

                def transpose_x():
                    for c in range(4):
                        for k in range(2):
                            for t in range(TT):
                                last = nc.tensor.transpose(
                                    ring_banks[c][:, k * SEQ + t * P:k * SEQ + (t + 1) * P],
                                    x[:, t, (2 * c + k) * P:(2 * c + k + 1) * P], ident[:, :])
                        last.then_inc(*xt_ps.one)

                def tile_by_x(slot, dst):
                    for k in range(KC):
                        w_hi, w_lo = hi[:, slot, k * P:(k + 1) * P], lo[:, slot, k * P:(k + 1) * P]
                        mm(dst, w_hi, xt[:, k, 0, :], start=k == 0, stop=False)
                        mm(dst, w_hi, xt[:, k, 1, :], start=False, stop=False)
                        last = mm(dst, w_lo, xt[:, k, 0, :], start=False, stop=k == KC - 1)
                    last.then_inc(*tile_used.one)

                def by_tile(slot, stationary, chunks, banks, first, final):
                    for t in range(TT):
                        for n, (k, col, c) in enumerate(chunks):
                            dst = banks[t][c][:, :]
                            begin = first and n < len(banks[t])
                            end = final and n >= len(chunks) - len(banks[t])
                            cols = slice(col, col + HALF)
                            mm(dst, stationary(0, t, k), hi[:, slot, cols], start=begin, stop=False)
                            mm(dst, stationary(0, t, k), lo[:, slot, cols], start=False, stop=False)
                            last = mm(dst, stationary(1, t, k), hi[:, slot, cols], start=False,
                                      stop=end)
                    last.then_inc(*tile_used.one)

                def x_part(part, t, k):
                    return xt[:, k, part, t * P:(t + 1) * P]

                def mixed_part(part, t, k):
                    return mixed[:, k, part, t * P:(t + 1) * P]

                model_banks = [[acc_banks[2 * t], acc_banks[2 * t + 1]] for t in range(TT)]

                pe.wait_ge(*x_ready(layer, 0))
                transpose_x()
                pe.wait_ge(*xt_lo(layer, 4))
                for n in range(AG0, QKV0):
                    pe.wait_ge(*lo_done[n % RING](layer, n // RING + 1))
                    tile_by_x(n % RING, bank[(4 + n) % 8][:, 0:SEQ])
                for g, (b, used_by) in enumerate(((4, 1), (6, 2), (0, 3))):
                    pe.wait_ge(*conv_u(layer, used_by))
                    for m in range(4):
                        n = QKV0 + 4 * g + m
                        pe.wait_ge(*lo_done[n % RING](layer, n // RING + 1))
                        by_tile(n % RING, x_part, [(2 * m, 0, 0), (2 * m + 1, HALF, 0)],
                                [[bank[b]], [bank[b + 1]]], m == 0, m == 3)
                pe.wait_ge(*conv_u(layer, CT))
                for c, (src, b) in enumerate(((q_sb, 2), (q_sb, 3), (k_sb, 4), (k_sb, 5))):
                    pe.wait_ge(*rotated(layer, 2 if c < 2 else 4))
                    for k in range(2):
                        pair = 2 * (c % 2) + k
                        for t in range(TT):
                            last = nc.tensor.transpose(
                                bank[b][:, k * SEQ + t * P:k * SEQ + (t + 1) * P],
                                src[:, t, pair * P:(pair + 1) * P], ident[:, :])
                    last.then_inc(*qk_ps.one)

                def scores(g):
                    if g >= 2:
                        pe.wait_ge(*sc_used(layer, g - 1))
                    rows = slice(DH * (g % 2), DH * (g % 2) + DH)
                    mm(bank[6 + g % 2][:, 0:P], q_t[rows, g // 2, 0:P], k_t[rows, g // 2, 0:P],
                       start=True, stop=True)
                    mm(bank[6 + g % 2][:, P:3 * P], q_t[rows, g // 2, P:2 * P],
                       k_t[rows, g // 2, :], start=True, stop=True).then_inc(*sc_ps.one)

                def probs_transposed(g):
                    pe.wait_ge(*pr_done(layer, g + 1))
                    if g >= 1:
                        pe.wait_ge(*pt_done(layer, g))
                    for c in range(3):
                        last = nc.tensor.transpose(bank[4][:, c * P:(c + 1) * P],
                                                   pr[:, g, c * P:(c + 1) * P], ident[:, :])
                    last.then_inc(*pt_ps.one)

                def weighted_values(pair):
                    if pair:
                        pe.wait_ge(*mix_lo(layer, pair))
                    for e in range(2):
                        g = 2 * pair + e
                        pe.wait_ge(*pt_done(layer, g + 1))
                        rows, cols = slice(DH * e, DH * e + DH), slice(g * DH, (g + 1) * DH)
                        mm(bank[5][rows, 0:SEQ], v_sb[:, 0, cols],
                           p_t[:, g, 0:2 * P], start=True, stop=False)
                        last = mm(bank[5][rows, P:SEQ], v_sb[:, 1, cols], p_t[:, g, 2 * P:3 * P],
                                  start=False, stop=True)
                    last.then_inc(*pv_ps.one)

                pe.wait_ge(*qk_done(layer, 4))
                scores(0)
                scores(1)
                pe.wait_ge(*acc_done(layer, 1))
                pe.wait_ge(*prod_used(layer, TAPS - 1))
                for c in range(CT):
                    last = mm(bank[3][:, 0:SEQ], ones[:, :], acc[:, c, :], start=c == 0,
                              stop=c == CT - 1)
                last.then_inc(*mean_ps.one)
                pe.wait_ge(*v_done(layer, TT))

                def project(m):
                    n = WO0 + m
                    k = (m + PAIRS) % KC
                    pe.wait_ge(*lo_done[n % RING](layer, n // RING + 1))
                    by_tile(n % RING, mixed_part, [(k, 0, 0), (k, HALF, 1)], model_banks,
                            m == 0, m == KC - 1)

                for g in range(HEADS):
                    probs_transposed(g)
                    if g + 2 < HEADS:
                        scores(g + 2)
                    if g == 0:
                        pe.wait_ge(*sq_done(layer, 1))
                        for c in range(CT):
                            last = mm(bank[2][:, 0:SEQ], ones[:, :], sq[:, c, :], start=c == 0,
                                      stop=c == CT - 1)
                        last.then_inc(*var_ps.one)
                    if g >= 2 and g % 2 == 0:
                        weighted_values(g // 2 - 1)
                    if g == 5:
                        pe.wait_ge(*mix_conv(layer, 1))
                    if g >= 5:
                        project(g - 5)
                project(3)
                weighted_values(PAIRS - 1)
                pe.wait_ge(*mix_lo(layer, PAIRS))
                for m in range(4, KC):
                    project(m)
                pe.wait_ge(*x1_ready(layer, TT))
                transpose_x()
                pe.wait_ge(*xt_lo(layer, 8))
                for n in range(WQ0, U0):
                    pe.wait_ge(*lo_done[n % RING](layer, n // RING + 1))
                    if n >= WQ0 + 8:
                        pe.wait_ge(*qp_done(layer, n - WQ0 - 7))
                    tile_by_x(n % RING, bank[n % 8][:, 0:SEQ])
                pe.wait_ge(*qp_done(layer, HC))
                pe.wait_ge(*keys_in(layer, 1))
                for t in range(TT):
                    for c in range(4):
                        for k in range(4):
                            g = 4 * c + k
                            last = mm(bank[4 * t + c][:, k * NK:(k + 1) * NK],
                                      qp_t[:, g, t * P:(t + 1) * P], keys_sb[:, g, :],
                                      start=True, stop=True)
                        last.then_inc(*sp_ps.one)

                def u_tile(i, j):
                    pe.wait_ge(*lo_done[j](layer, i + (U0 // RING + 1)))
                    pe.wait_ge(*gelu_done(layer, RING * i + (j - RING + 1)))
                    tile_by_x(j, ring_banks[j][:, 0:SEQ])

                def gate_matrices(seg, i, j):
                    pe.wait_ge(*gated_done(layer, seg * GROUPS + RING * i + (j + 1)))
                    pe.wait_ge(*w_done(layer, seg * GROUPS + RING * i + (j - 1)))
                    b = j % 2
                    for t in range(GROUP):
                        dst = (acc_banks, ring_banks)[seg][b][:, t * SEG:(t + 1) * SEG]
                        for part in range(PARTS):
                            last = mm(dst, one_b[:, b, t, :], gated_a[:, b, part, t, :],
                                      start=part == 0, stop=part == PARTS - 1)
                    last.then_inc(*g_ps.one)

                pe.wait_ge(*s_done(layer, TT * 4))
                pe.sem_inc(pe_held, 1)
                with pe.Fori(0, TOP_TURNS + 1) as i:
                    for j in range(RING):
                        u_tile(i, j)
                pe.wait_ge(*chosen(layer, 1))
                for t in range(TT):
                    for c, src in enumerate((e1, e2, gate)):
                        last = nc.tensor.transpose(
                            bank[t][:, c * P:(c + 1) * P],
                            src[:, t].rearrange("p g k -> p (g k)"), ident[:, :])
                    last.then_inc(*chosen_ps.one)
                with pe.Fori(TOP_TURNS + 1, G_TURN) as i:
                    for j in range(RING):
                        u_tile(i, j)
                with pe.Fori(0, TURNS - G_TURN) as i:
                    for j in range(RING):
                        u_tile(i + G_TURN, j)
                        gate_matrices(0, i, j)

                def v_turn(i, first=False, final=False, gates=False):
                    for j in range(RING):
                        pe.wait_ge(*lo_done[j](layer, i + (V0 // RING + 1)))
                        pe.wait_ge(*wlo_done(layer, RING * i + (j + 1)))
                        by_tile(j, lambda part, t, k, j=j: ws[:, j, part, t * P:(t + 1) * P],
                                [(0, 0, 0), (0, HALF, 1)], model_banks,
                                first and j == 0, final and j == RING - 1)
                        if gates:
                            gate_matrices(1, i, j)

                pe.wait_ge(*gelu_done(layer, NK))
                v_turn(0, first=True, gates=True)
                with pe.Fori(1, G_TURN) as i:
                    v_turn(i, gates=True)
                with pe.Fori(G_TURN, LAST) as i:
                    v_turn(i)
                v_turn(LAST, final=True)


def rope_table():
    inv = np.power(np.float32(10000.0), -np.arange(0, DH, 2, dtype=np.float32) / DH)
    ang = np.arange(SEQ, dtype=np.float32)[:, None] * inv[None, :].astype(np.float32)
    cos, sin = np.cos(ang), np.sin(ang)
    both = np.stack([np.concatenate([cos, cos], 1), np.concatenate([-sin, sin], 1)], 1)
    return both.reshape(TT, P, 2, DH).transpose(1, 0, 2, 3).astype(np.float32)


def causal_table():
    tri = np.where(np.arange(P)[None, :] <= np.arange(P)[:, None], 0.0, MASKED)
    return np.concatenate([tri, np.zeros((P, P)), tri], 1).astype(np.float32)


def kernel(x, w_in, conv_w, conv_b, conv_ln_g, conv_ln_b, w_out, ln1_g, ln1_b,
           peer_wq, peer_keys, peer_u, peer_v, ln2_g, ln2_b):
    import concourse.bacc as bacc
    from concourse.bass_utils import run_bass_kernel_spmd

    w_in, w_out, peer_wq, peer_u, peer_v = map(np.asarray, (w_in, w_out, peer_wq, peer_u, peer_v))
    L = DEPTH
    ag = w_in[:, :, 3 * AW:].reshape(L, KC, P, 2, CT, P).transpose(0, 4, 3, 2, 1, 5)
    qkv = w_in[:, :, :3 * AW].reshape(L, KC // 2, 2, P, 3, AW).transpose(0, 4, 1, 3, 2, 5)
    wo = np.concatenate([w_out[:, AW:], w_out[:, :AW]], axis=1)
    wq = peer_wq.reshape(L, KC, P, HC, P).transpose(0, 3, 2, 1, 4)
    u = peer_u.reshape(L, NK, NK, KC, P).transpose(0, 1, 4, 3, 2)
    stream = np.concatenate([ag.reshape(L, -1, D), qkv.reshape(L, -1, D), wo,
                             wq.reshape(L, -1, D), u.reshape(L, -1, D),
                             peer_v.reshape(L, -1, D)], axis=1).reshape(-1, D)
    keys_t = np.asarray(peer_keys).transpose(0, 4, 1, 2, 3).reshape(L * P, HC * NK)
    conv_p = np.concatenate([np.asarray(conv_w), np.asarray(conv_b)[:, None],
                             np.asarray(conv_ln_g)[:, None], np.asarray(conv_ln_b)[:, None]], 1)
    conv_p = conv_p.reshape(L, TAPS + 3, CT, P).transpose(0, 3, 2, 1).reshape(L * P, -1)
    ln_p = np.stack([np.asarray(a) for a in (ln1_g, ln1_b, ln2_g, ln2_b)], 1).reshape(L * 4, D)
    arrays = {
        "x": np.asarray(x).reshape(SEQ, D), "stream": stream, "keys_t": keys_t, "conv_p": conv_p,
        "ln_p": ln_p, "rope": rope_table().reshape(P, -1), "causal": causal_table(),
    }
    arrays = {name: np.ascontiguousarray(a) for name, a in arrays.items()}

    nc = bacc.Bacc("TRN2", target_bir_lowering=False, num_devices=1)
    args = [nc.dram_tensor(f"in_{name}", a.shape, mybir.dt.float32, kind="ExternalInput").ap()
            for name, a in arrays.items()]
    result = nc.dram_tensor("result", (SEQ, D), mybir.dt.float32, kind="ExternalOutput").ap()
    x1_dram = nc.dram_tensor("x1_kept", (SEQ, D), mybir.dt.float32, kind="Internal").ap()
    build(nc, *args, x1_dram, result)
    r = run_bass_kernel_spmd(nc, [{f"in_{name}": a for name, a in arrays.items()}], core_ids=[0])
    return np.asarray(r.results[0]["result"]).reshape(1, SEQ, D)
```

```python
from contextlib import ExitStack

import numpy as np
import concourse.bass as bass
from concourse import mybir

P = 128
SEQ, D, DEPTH = 256, 1024, 2
HEADS, DH = 8, 64
AW = HEADS * DH
CW = D - AW
TAPS = 31
PH, NK, TOPK = 8, 128, 16
HC = 2 * PH
ALPHA = (2 * DEPTH) ** 0.25
EPS = 1e-5
SCALE = DH ** -0.5
MASKED = -1e30
LOWEST = -3e38

TT = SEQ // P
KC = D // P
CT = CW // P
PAIRS = HEADS // 2
HALF = D // 2

AG0 = 0
QKV0 = AG0 + 2 * CT
WO0 = QKV0 + 3 * (KC // 2)
WQ0 = WO0 + KC
U0 = WQ0 + HC
V0 = U0 + NK
TILES = V0 + NK
RING = 4
HI_LEAD, LO_LEAD = 3, 2
WHI_LEAD, WLO_LEAD = 2, 1
GROUP = 4
GROUPS = SEQ // GROUP
assert GROUPS == NK // 2
PROD_RING = 3
LATE_TAPS = 3
LATE_PLAN = (0, 0, 0, 0, 0, 0, 3, 0)
POOL_TAPS = TAPS - LATE_TAPS
assert sum(LATE_PLAN) == LATE_TAPS and (POOL_TAPS - 1) % PROD_RING == 0
DVE_TAPS = ((0, 0, 1, 1, 1, 1, 1, 1), (2, 2, 2, 2, 2, 0, 1, 2, 2, 0, 1, 1), (4,), (2, 2, 0, 0, 0, 0, 0, 0))
ACT_TAPS = ((0,) * 8, (2, 1) * 6, (2,), (2, 2, 2, 2, 0, 0, 0, 0))
PE_TAPS = ((0,) * 8, (0,) * 12, (7,), (4, 4, 4, 4, 4, 4, 0, 0))
assert all(sum(map(sum, plan)) == n for plan, n in ((DVE_TAPS, TAPS), (ACT_TAPS, POOL_TAPS),
                                                    (PE_TAPS, TAPS)))
PROBS_RING = 4
TURNS = NK // RING
LAST = TURNS - 1
TOP_GROUPS = 8
A_TURNS = TT * HC // TOP_GROUPS
PAIR_HEADS = 2
B_TURNS = PH // PAIR_HEADS
C_TURNS = PH // PAIR_HEADS
TOP_TURNS = A_TURNS + B_TURNS + C_TURNS
G_TURN = TURNS // 2
PARTS = 3
SEG = NK // 2
WIDE, NARROW = 4, 4
WIDE_SUMS = WIDE * TOPK
SUMS = WIDE_SUMS + (TOPK - WIDE) * NARROW
assert (WIDE + 1) * (NARROW + 1) > TOPK
DVE_STEPS = 478


class Signal:

    def __init__(self, ctx, nc, name, per_layer, unit=1, primed=0):
        self.sem = ctx.enter_context(nc.semaphore(name))
        self.per_layer, self.unit, self.primed = per_layer, unit, primed
        self.one = (self.sem, unit)

    def __call__(self, layer, k):
        return self.sem, (layer * self.per_layer + k + self.primed) * self.unit


class Steps:

    def __init__(self, engine, sem, base, per_turn):
        self.engine, self.sem, self.per_turn = engine, sem, per_turn
        self.base, self.n = base, 0

    def __call__(self, instruction):
        instruction.then_inc(self.sem, 1)
        self.n += 1
        return self.n

    def settle(self, n=None):
        self.engine.wait_ge(self.sem, self.base + (self.n if n is None else n))

    def settle_alone(self, held):
        self.settle()
        self.engine.sem_inc(held, 1)

    def turn(self, i, per_turn):
        return Steps(self.engine, self.sem, self.base + self.n + i * per_turn, per_turn)

    def ended(self, turn, turns=1):
        assert turn.n == turn.per_turn, (turn.n, turn.per_turn)
        self.n += turns * turn.n


def build(nc, x_in, stream, keys_t, conv_p, ln_p, rope, causal, x1_dram, out):
    f32, f32r, u32, bf16 = (mybir.dt.float32, mybir.dt.float32r, mybir.dt.uint32,
                            mybir.dt.bfloat16)
    ALU, ACT = mybir.AluOpType, mybir.ActivationFunctionType
    X = mybir.AxisListType.X
    ds = bass.ds

    ctx = ExitStack()
    with ctx:
        start = (nc.sbuf_base + 31) // 32 * 32
        used = [start]

        def place(name, shape, dt=f32, at=None):
            size = int(np.prod(shape[1:])) * (2 if dt == bf16 else 4)
            if at is None:
                at = used[0]
                used[0] += size
            return nc.alloc_sbuf_tensor_at(name, shape, dt, offset=at)

        raw = place("raw", [P, RING, D])
        hi = place("hi", [P, RING, D], f32r)
        lo = place("lo", [P, RING, D], f32r)
        x_at = used[0]
        x = place("x", [P, TT, D])
        gated_a = place("gated_a", [P, 2, PARTS, GROUP, SEG], bf16, at=x_at)
        one_b = place("onehot_b", [P, 2, GROUP, NK], bf16, at=x_at + 3072)
        one_a = place("onehot_a", [P, 2, GROUP, SEG], bf16, at=x_at + 5120)
        ident = place("ident", [P, P])
        iota = place("iota", [P, P])
        i1_t = place("i1_t", [P, SEQ])
        i2_t = place("i2_t", [P, SEQ])
        gate_part = place("gate_part", [P, PARTS, SEQ], bf16)
        gate_rest = place("gate_rest", [P, PARTS - 1, P])
        xt_at = used[0]
        xt = place("xt", [P, KC, 2, SEQ], f32r)
        ws = place("w_split", [P, RING, 2, SEQ], f32r, at=xt_at)
        ones = place("ones", [P, P])
        small = place("small", [P, 160])
        act = used[0]
        h = place("h", [P, NK * SEQ])
        assert used[0] <= nc.sbuf_top, used[0]
        h_tok = h[:, :].rearrange("p (b t) -> p t b", t=SEQ)

        def inside(name, at, shape, dt=f32):
            assert at + int(np.prod(shape[1:])) * 4 <= NK * SEQ * 4
            return place(name, shape, dt, at=act + at)

        ln2_g, ln2_b = inside("ln2_g", 0, [P, D]), inside("ln2_b", 4096, [P, D])
        ln1_g, ln1_b = inside("ln1_g", 8192, [P, D]), inside("ln1_b", 12288, [P, D])
        rope_sb = inside("rope_sb", 16384, [P, TT, 2, DH])
        causal_sb = inside("causal_sb", 17408, [P, 3 * P])
        conv_sb = inside("conv_sb", 18944, [P, CT, TAPS + 3])
        u_pad = inside("u_pad", 19968, [P, CT, 288])
        acc = inside("conv_acc", 24576, [P, CT, SEQ])
        xc = inside("conv_centred", 28672, [P, CT, SEQ])
        sq = inside("conv_squares", 32768, [P, CT, SEQ])
        prod = inside("conv_products", 28672, [P, PROD_RING, 2, SEQ])
        sg = inside("sigmoid", 36864, [P, CT, SEQ])
        rstd = inside("conv_rstd", 40960, [P, 2, SEQ])
        q_sb = inside("q_rotated", 43008, [P, TT, AW])
        k_sb = inside("k_rotated", 47104, [P, TT, AW])
        m1, m2 = inside("rope_cos_part", 51200, [P, AW]), inside("rope_sin_part", 53248, [P, AW])
        v_sb = inside("v", 55296, [P, TT, AW])
        q_t = inside("q_t", 59392, [P, PAIRS, SEQ])
        k_t = inside("k_t", 63488, [P, PAIRS, SEQ])
        sm = inside("masked_scores", 67584, [P, PROBS_RING, 3 * P])
        pr = inside("probs", 73728, [P, PROBS_RING, 3 * P])
        p_t = inside("probs_t", 79872, [P, PROBS_RING, 3 * P])
        diag = inside("tap_diagonals", 86016, [P, TAPS, P])
        mixed = inside("mixed", 104448, [P, KC, 2, SEQ], f32r)
        res = inside("residual", 120832, [P, TT, D])
        qp_t = inside("peer_q_t", 19968, [P, HC, SEQ])
        keys_sb = inside("keys_sb", 67584, [P, HC, NK])
        s_at = (NK * 3 // 4) * SEQ * 4
        s_sb = inside("scores", s_at, [P, TT * HC * NK])
        t0 = s_at + TT * HC * NK * 4
        sg_in = inside("topk_in", t0, [P, TOP_GROUPS, NK])
        sg_rest = inside("topk_rest", t0 + 4096, [P, TOP_GROUPS, NK])
        top_v8 = inside("top_values_now", t0 + 8192, [P, TOP_GROUPS, TOPK])
        top_i8 = inside("top_index_now", t0 + 8704, [P, TOP_GROUPS, TOPK], u32)
        top_v = inside("top_values", t0 + 9216, [P, TT, HC, TOPK])
        top_i = inside("top_index", t0 + 11264, [P, TT, HC, TOPK])
        best_v = inside("best_values", t0 + 13312, [P, TT, PH, TOPK])
        best_c = inside("best_places", t0 + 14336, [P, TT, PH, TOPK], u32)
        gate = inside("gates", t0 + 15360, [P, TT, PH, TOPK])
        comb = inside("pair_sums", t0, [P, PAIR_HEADS * TT, SUMS])
        comb_rest = inside("pair_sums_rest", t0 + 4096, [P, PAIR_HEADS * TT, SUMS])
        cmp = inside("place_matches", t0, [P, 2, TT, TOPK, TOPK])
        hit = inside("matched_keys", t0 + 4096, [P, 2, TT, TOPK, TOPK])
        def late(name, n, dt=f32):
            return inside(name, s_at + 1024 * n, [P, TT, PH, TOPK], dt)

        e1, e2, row_u, col_u = late("first_keys", 0), late("second_keys", 1), late("row_place", 2, u32), late("column_place", 3, u32)
        row_f, col_f, narrow_u, narrow_f = late("row_place_f", 4), late("column_place_f", 5), late("narrow_place", 6, u32), late("narrow_place_f", 7)
        is_narrow, place_f = late("is_narrow", 8), late("place_f", 9)
        best_v4 = inside("best_values_now", s_at + 10240, [P, PAIR_HEADS * TT, TOPK])
        best_c4 = inside("best_places_now", s_at + 10496, [P, PAIR_HEADS * TT, TOPK], u32)
        gate_sum = inside("gate_sums", s_at + 10752, [P, TT, PH])
        gate_inv = inside("gate_inverses", s_at + 10816, [P, TT, PH])

        cut = [0]

        def piece(n):
            cut[0] += n
            assert cut[0] <= 160
            return small[:, cut[0] - n:cut[0]]

        row_max, neg_max, row_sum, row_inv = piece(16), piece(16), piece(16), piece(16)
        ln_bias = piece(2)
        ln_stats, ln_mv, ln_std, ln_rstd = piece(24), piece(4), piece(2), piece(2)

        bank = [ctx.enter_context(nc.psum_tensor(f"bank{n}", [P, 512], f32)) for n in range(8)]
        acc_banks = bank[0:4]
        ring_banks = bank[4:8]
        ag_banks = [bank[2 * c:2 * c + 2] for c in range(CT)]
        conv_bank = bank[2]
        pt_bank, pv_bank, mean_bank, var_bank = bank[4:8]
        score_banks = bank[6:8]

        def signal(name, per_layer, unit=1, primed=0):
            return Signal(ctx, nc, name, per_layer, unit, primed)

        raw_in = [signal(f"raw_in{j}", TILES // RING, 16) for j in range(RING)]
        hi_done = signal("hi_done", TILES)
        lo_done = [signal(f"lo_done{j}", TILES // RING) for j in range(RING)]
        tile_used = signal("tile_used", TILES, primed=RING)
        x_loaded = [signal(f"x_loaded{t}", 1, 16) for t in range(TT)]
        consts_made = signal("consts_made", 1)
        pool_setup = signal("pool_setup", 1)
        x_ready = signal("x_ready", 2 * TT, primed=2 * TT)
        xt_used = signal("first_chunks_used", 1)
        first_summed = signal("first_tokens_summed", 2)
        params_in = signal("params_in", 5, 16)
        keys_in = signal("keys_in", 1, 16)
        ln2_in = signal("ln2_params_in", 2, 16)
        xt_ps, xt_hi, xt_lo = signal("xt_ps", 8), signal("xt_hi", 8), signal("xt_lo", 8)
        sig_done, conv_u = signal("sigmoid_done", CT), signal("conv_u", CT)
        rotated, v_done = signal("rotated", 2 * TT), signal("v_done", TT)
        qk_ps, qk_done = signal("qk_t_ps", 4), signal("qk_t_done", 4)
        sc_ps, sc_used = signal("scores_ps", HEADS), signal("scores_masked", HEADS)
        max_done, exp_done = signal("max_done", HEADS), signal("exp_done", 2 * HEADS)
        pr_done, pt_ps = signal("probs_done", HEADS), signal("probs_t_ps", HEADS)
        pt_done, pv_ps = signal("probs_t_done", HEADS), signal("pv_ps", PAIRS)
        mix_hi, mix_lo = signal("mixed_hi", PAIRS), signal("mixed_lo", PAIRS)
        mix_conv_hi, mix_conv = signal("mixed_conv_hi", CT), signal("mixed_conv", CT)
        acc_done, mean_ps = signal("conv_done", 1), signal("conv_mean_ps", 1)
        centred, sq_done = signal("conv_centred_done", 1), signal("conv_squares_done", 1)
        var_ps, var_done = signal("conv_var_ps", 1), signal("conv_var_done", 1)
        std_done, normed = signal("conv_std_done", 1), signal("conv_normed", CT)
        silu_done = signal("silu_done", CT)
        ln_var, ln_root = signal("ln_var", 2 * TT), signal("ln_root", 2 * TT)
        x1_ready = signal("x1_ready", 2 * TT)
        x1_kept, x1_back = signal("x1_in_dram", TT, 16), signal("x1_back", TT, 16)
        conv_first, prod_done = signal("conv_first_tap", 1), signal("conv_product", POOL_TAPS - 1)
        prod_used = signal("conv_product_added", POOL_TAPS - 1)
        diags_made, conv_ps = signal("tap_diagonals_made", 1), signal("conv_ps", 1)
        conv_out = signal("conv_ps_out", 1)
        qp_done, sp_ps = signal("peer_q_done", HC), signal("peer_scores_ps", TT * 4)
        s_done = signal("peer_scores_done", TT * 4)
        top_in, top_in_used = signal("topk_in_ready", A_TURNS), signal("topk_in_used", A_TURNS)
        best_done, gate_exp = signal("best_done", 1), signal("gate_exp", 1)
        chosen, chosen_ps = signal("chosen", 1), signal("chosen_t_ps", TT)
        tables = signal("chosen_tables", TT)
        gelu_done = signal("gelu_done", NK, primed=RING)
        one_done, gated_done = signal("onehots_done", NK), signal("gated_done", NK)
        g_ps, w_done = signal("gate_matrix_ps", NK), signal("w_done", NK, primed=2)
        whi_done, wlo_done = signal("w_hi_done", NK), signal("w_lo_done", NK)
        out_done = signal("out_done", 1, 16)
        pe_held = ctx.enter_context(nc.semaphore("pe_held"))
        dve_held = ctx.enter_context(nc.semaphore("dve_held"))
        pool_held = ctx.enter_context(nc.semaphore("pool_held"))
        dve_steps = ctx.enter_context(nc.semaphore("dve_steps"))

        block = ctx.enter_context(nc.Block())

        @block.sync
        def _(sp):
            for t in range(TT):
                sp.dma_start(x[:, t, :], x_in[t * P:(t + 1) * P, :]).then_inc(*x_loaded[t].one)
            for j in range(RING):
                sp.dma_start(raw[:, j, :], stream[j * P:(j + 1) * P, :]).then_inc(*raw_in[j].one)
            with sp.Fori(1, DEPTH * TILES // RING) as turn:
                for j in range(RING):
                    sp.wait_ge(*lo_done[j](0, turn))
                    sp.dma_start(raw[:, j, :], stream[ds((RING * turn + j) * P, P), :])\
                      .then_inc(*raw_in[j].one)
            for t in range(TT):
                for c in range(2):
                    cols = slice(c * HALF, (c + 1) * HALF)
                    sp.wait_ge(*x_ready(DEPTH - 1, 2 * t + c + 1))
                    sp.dma_start(out[t * P:(t + 1) * P, cols], x[:, t, cols])\
                      .then_inc(*out_done.one)
            sp.wait_ge(*out_done(0, 2 * TT))

        @block.gpsimd
        def _(pool):
            nc.gpsimd.iota(iota[:, :], pattern=[[1, P]], base=0, channel_multiplier=0,
                           allow_small_or_imprecise_dtypes=True)
            nc.gpsimd.memset(ones[:, :], 1.0 / CW)
            nc.gpsimd.memset(ident[:, :], 0.0).then_inc(*pool_setup.one)
            pool.wait_ge(*pool_setup(0, 1))
            nc.gpsimd.affine_select(out=ident[:, :], in_=ident[:, :], compare_op=ALU.not_equal,
                                    fill=1.0, base=0, pattern=[[-1, P]], channel_multiplier=1)\
              .then_inc(*consts_made.one)
            for _ in range(2):
                pool.sem_inc(w_done.sem, 1)
            with pool.Fori(0, DEPTH) as layer:
                def rest(turn, j):
                    pool.wait_ge(*hi_done(layer, RING * turn + (j + 1)))
                    nc.gpsimd.tensor_tensor(lo[:, j, :], raw[:, j, :], hi[:, j, :].bitcast(f32),
                                            ALU.subtract).then_inc(*lo_done[j].one)

                for j in range(LO_LEAD):
                    rest(AG0 // RING, j)
                pool.wait_ge(*x_ready(layer, 0))
                pool.wait_ge(*params_in(layer, 5))
                nc.gpsimd.tensor_tensor(
                    diag[:, :, :], ident[:, None, :].to_broadcast([P, TAPS, P]),
                    conv_sb[:, 3, 0:TAPS][:, :, None].to_broadcast([P, TAPS, P]), ALU.mult)\
                  .then_inc(*diags_made.one)
                pool.wait_ge(*conv_first(layer, 1))
                pool.sem_inc(pool_held, 1)
                with pool.Fori(0, (POOL_TAPS - 1) // PROD_RING) as i:
                    for c in range(PROD_RING):
                        pool.wait_ge(*prod_done(layer, PROD_RING * i + (c + 1)))
                        if c:
                            pool.wait_ge(*prod_used(layer, PROD_RING * i + c))
                        nc.gpsimd.tensor_tensor(acc[:, 1:3, :], acc[:, 1:3, :], prod[:, c, :, :],
                                                ALU.add).then_inc(*prod_used.one)
                    pool.wait_ge(*prod_used(layer, PROD_RING * i + PROD_RING))
                    pool.sem_inc(pool_held, 1)

                for n in range(WO0 + LO_LEAD, WQ0 + LO_LEAD):
                    rest(n // RING, n % RING)
                pool.sem_inc(pool_held, 1)
                with pool.Fori(U0 // RING, U0 // RING + TOP_TURNS) as turn:
                    rest(turn, 3)
                    rest(turn + 1, 0)
                    rest(turn + 1, 1)

                def gated(seg, i, j):
                    pool.wait_ge(*one_done(layer, seg * GROUPS + RING * i + (j + 1)))
                    tok, b = ds(i * (RING * GROUP) + j * GROUP, GROUP), j % 2
                    for part in range(PARTS):
                        last = nc.gpsimd.tensor_tensor(
                            gated_a[:, b, part], one_a[:, b],
                            gate_part[:, part, tok][:, :, None].to_broadcast([P, GROUP, SEG]),
                            ALU.mult)
                    last.then_inc(*gated_done.one)

                with pool.Fori(0, TURNS - G_TURN) as i:
                    for j in range(RING):
                        gated(0, i, j)

                def w_rest(i, j):
                    pool.wait_ge(*whi_done(layer, RING * i + (j + 1)))
                    nc.gpsimd.tensor_tensor(
                        ws[:, j, 1, :], h[:, ds(i * (RING * SEQ) + j * SEQ, SEQ)],
                        ws[:, j, 0, :].bitcast(f32), ALU.subtract).then_inc(*wlo_done.one)

                with pool.Fori(0, G_TURN) as i:
                    for j in range(RING):
                        gated(1, i, j)
                        w_rest(i, j)
                with pool.Fori(G_TURN, TURNS) as i:
                    for j in range(RING):
                        w_rest(i, j)

        @block.scalar
        def _(act):
            act.wait_ge(*consts_made(0, 1))
            for _ in range(RING):
                act.sem_inc(gelu_done.sem, 1)
            with act.Fori(0, DEPTH) as layer:

                def head(turn, j):
                    turn, j = turn + j // RING, j % RING
                    act.wait_ge(*raw_in[j](layer, turn + 1))
                    act.wait_ge(*tile_used(layer, RING * turn + (j - RING + 1)))
                    nc.scalar.activation(hi[:, j, :], raw[:, j, :], ACT.Copy).then_inc(*hi_done.one)

                def x_heads(done):
                    for c in range(4):
                        act.wait_ge(*xt_ps(layer, done + c + 1))
                        nc.scalar.activation(
                            xt[:, 2 * c:2 * c + 2, 0, :],
                            ring_banks[c][:, :].rearrange("p (k t) -> p k t", k=2), ACT.Copy)\
                          .then_inc(*xt_hi.one)

                def root(which, t):
                    act.wait_ge(*ln_var(layer, TT * which + t + 1))
                    nc.scalar.activation(ln_std[:, t:t + 1], ln_mv[:, 2 * t + 1:2 * t + 2],
                                         ACT.Sqrt).then_inc(*ln_root.one)

                head(0, 0)
                x_heads(0)
                for n in range(1, HI_LEAD):
                    head(0, n)
                act.dma_start(conv_sb[:, :, :], conv_p[ds(layer * P, P), :])\
                   .then_inc(*params_in.one)
                act.dma_start(rope_sb[:, :, :, :], rope).then_inc(*params_in.one)
                act.dma_start(causal_sb[:, :], causal).then_inc(*params_in.one)
                act.dma_start(ln1_g[:, :], ln_p[ds(layer * 4, 1), :].to_broadcast([P, D]))\
                   .then_inc(*params_in.one)
                act.dma_start(ln1_b[:, :], ln_p[ds(layer * 4 + 1, 1), :].to_broadcast([P, D]))\
                   .then_inc(*params_in.one)

                def qk_transposed(c):
                    act.wait_ge(*qk_ps(layer, c + 1))
                    nc.scalar.activation((q_t, k_t)[c // 2][:, 2 * (c % 2):2 * (c % 2) + 2, :],
                                         bank[(6, 7, 0, 1)[c]][:, :]
                                         .rearrange("p (k t) -> p k t", k=2),
                                         ACT.Copy).then_inc(*qk_done.one)

                for n in range(AG0, QKV0):
                    head(0, n + HI_LEAD)
                    c = (n - AG0) // 2
                    if (n - AG0) % 2:
                        act.wait_ge(*tile_used(layer, n + 1))
                        nc.scalar.activation(sg[:, c, :], ag_banks[c][1][:, 0:SEQ],
                                             ACT.Sigmoid).then_inc(*sig_done.one)
                act.wait_ge(*params_in(layer, 5))

                taps_done = [0]

                def conv_products(count):
                    for tap in range(taps_done[0], taps_done[0] + count):
                        if tap > PROD_RING:
                            act.wait_ge(*prod_used(layer, tap - PROD_RING))
                        for c in range(2):
                            window = u_pad[:, 1 + c, tap:tap + SEQ]
                            weight = conv_sb[:, 1 + c, tap:tap + 1]
                            if tap == 0:
                                end = nc.scalar.activation(
                                    acc[:, 1 + c, :], window, ACT.Identity, scale=weight,
                                    bias=conv_sb[:, 1 + c, TAPS:TAPS + 1])
                            else:
                                end = nc.scalar.activation(prod[:, (tap - 1) % PROD_RING, c, :],
                                                           window, ACT.Copy, scale=weight)
                        end.then_inc(*(conv_first if tap == 0 else prod_done).one)
                    taps_done[0] += count

                for m, count in enumerate(ACT_TAPS[1]):
                    head(0, QKV0 + m + HI_LEAD)
                    if m == 0:
                        act.wait_ge(*conv_u(layer, 3))
                    conv_products(count)
                    if QKV0 + m == WO0 - 2:
                        qk_transposed(0)
                        qk_transposed(1)
                qk_transposed(2)
                qk_transposed(3)
                for t in range(TT):
                    nc.scalar.activation(v_sb[:, t, :], bank[4 + t][:, :], ACT.Copy)\
                      .then_inc(*v_done.one)

                def probs_transposed(g):
                    act.wait_ge(*pt_ps(layer, g + 1))
                    nc.scalar.activation(p_t[:, g % PROBS_RING, :], pt_bank[:, 0:3 * P], ACT.Copy)\
                      .then_inc(*pt_done.one)

                def pv_heads(pair):
                    act.wait_ge(*pv_ps(layer, pair + 1))
                    nc.scalar.activation(mixed[:, pair, 0, :], pv_bank[:, 0:SEQ], ACT.Copy)\
                      .then_inc(*mix_hi.one)

                def exps(g):
                    act.wait_ge(*max_done(layer, g + 1))
                    slot = g % PROBS_RING
                    for t, (c0, c1) in enumerate(((0, P), (P, 3 * P))):
                        nc.scalar.activation(pr[:, slot, c0:c1], sm[:, slot, c0:c1], ACT.Exp,
                                             bias=neg_max[:, 2 * g + t:2 * g + t + 1], scale=SCALE,
                                             accum_out=row_sum[:, 2 * g + t:2 * g + t + 1])\
                          .then_inc(*exp_done.one)

                conv_products(ACT_TAPS[2][0])
                exps(0)
                for g, count in enumerate(ACT_TAPS[3]):
                    if g >= 1:
                        probs_transposed(g - 1)
                    if g == HEADS - 2:
                        act.wait_ge(*conv_ps(layer, 1))
                        nc.scalar.activation(acc[:, 3, :], conv_bank[:, 0:SEQ], ACT.Identity,
                                             scale=1.0, bias=conv_sb[:, 3, TAPS:TAPS + 1])\
                          .then_inc(*conv_out.one)
                    if g + 1 < HEADS:
                        exps(g + 1)
                    if g >= 3 and g % 2:
                        pv_heads(g // 2 - 1)
                    if g == HEADS - 2:
                        head(0, WO0 + HI_LEAD)
                    conv_products(count)
                probs_transposed(HEADS - 1)
                pv_heads(PAIRS - 1)
                act.wait_ge(*pt_ps(layer, HEADS))
                act.dma_start(keys_sb[:, :, :], keys_t[ds(layer * P, P), :]).then_inc(*keys_in.one)
                head(0, WO0 + 1 + HI_LEAD)
                act.wait_ge(*centred(layer, 1))
                nc.scalar.activation(sq[:, :, :], xc[:, :, :], ACT.Square)\
                  .then_inc(*sq_done.one)
                act.wait_ge(*var_done(layer, 1))
                nc.scalar.activation(rstd[:, 0, :], rstd[:, 1, :], ACT.Sqrt)\
                  .then_inc(*std_done.one)
                nc.scalar.preload_act_table(ACT.Silu)
                head(0, WO0 + 2 + HI_LEAD)
                head(0, WO0 + 3 + HI_LEAD)
                for c in range(CT):
                    act.wait_ge(*normed(layer, c + 1))
                    nc.scalar.activation(sq[:, c, :], xc[:, c, :], ACT.Silu,
                                         bias=conv_sb[:, c, TAPS + 2:TAPS + 3],
                                         scale=conv_sb[:, c, TAPS + 1:TAPS + 2])\
                      .then_inc(*silu_done.one)
                    act.wait_ge(*silu_done(layer, c + 1))
                    nc.scalar.activation(mixed[:, PAIRS + c, 0, :], sq[:, c, :], ACT.Copy)\
                      .then_inc(*mix_conv_hi.one)
                    if c == 0:
                        head(0, WO0 + 4 + HI_LEAD)
                nc.scalar.preload_act_table(ACT.Sqrt)
                root(0, 0)
                for n in range(WO0 + 5, WQ0):
                    head(0, n + HI_LEAD)
                root(0, 1)
                x_heads(4)
                act.wait_ge(*x1_ready(layer, 2 * TT))
                for t in range(TT):
                    act.dma_start(x1_dram[t * P:(t + 1) * P, :], x[:, t, :]).then_inc(*x1_kept.one)
                for n in range(WQ0, U0):
                    head(0, n + HI_LEAD)
                    act.wait_ge(*tile_used(layer, n + 1))
                    nc.scalar.activation(qp_t[:, n - WQ0, :], bank[n % 8][:, 0:SEQ], ACT.Copy)\
                      .then_inc(*qp_done.one)
                for c in range(TT * 4):
                    act.wait_ge(*sp_ps(layer, c + 1))
                    nc.scalar.activation(s_sb[:, c * 512:(c + 1) * 512], bank[(4 + c) % 8][:, :],
                                         ACT.Copy)\
                      .then_inc(*s_done.one)

                nc.scalar.preload_act_table(ACT.Gelu)

                def u_turn(i, before_last=None):
                    for j in range(RING):
                        head(i + U0 // RING, j + HI_LEAD)
                        if before_last and j == RING - 1:
                            before_last()
                        act.wait_ge(*tile_used(layer, RING * i + (U0 + j + 1)))
                        nc.scalar.activation(h[:, ds(i * (RING * SEQ) + j * SEQ, SEQ)],
                                             ring_banks[j][:, 0:SEQ], ACT.Gelu)\
                          .then_inc(*gelu_done.one)

                def stage(i):
                    size = TOP_GROUPS * NK
                    nc.scalar.activation(sg_in[:, :, :].rearrange("p g k -> p (g k)"),
                                         s_sb[:, ds(i * size, size)], ACT.Copy)\
                      .then_inc(*top_in.one)

                act.wait_ge(*s_done(layer, TT * 4))
                stage(0)
                with act.Fori(0, A_TURNS - 1) as i:
                    u_turn(i)
                    act.wait_ge(*top_in_used(layer, i + 1))
                    stage(i + 1)
                with act.Fori(A_TURNS - 1, A_TURNS + B_TURNS) as i:
                    u_turn(i)
                act.wait_ge(*best_done(layer, 1))
                nc.scalar.activation(gate[:, :, :, :], gate[:, :, :, :], ACT.Exp)\
                  .then_inc(*gate_exp.one)
                nc.scalar.preload_act_table(ACT.Gelu)
                with act.Fori(A_TURNS + B_TURNS, G_TURN) as i:
                    u_turn(i)
                act.wait_ge(*tables(layer, TT))
                with act.Fori(G_TURN, LAST) as i:
                    u_turn(i)

                def w_head(i, j):
                    i, j = i + j // RING, j % RING
                    act.wait_ge(*tile_used(layer, RING * i + (V0 + j - RING + 1)))
                    nc.scalar.activation(ws[:, j, 0, :], h[:, ds(i * (RING * SEQ) + j * SEQ, SEQ)],
                                         ACT.Copy).then_inc(*whi_done.one)

                def first_w_heads():
                    act.wait_ge(*w_done(layer, GROUPS))
                    act.wait_ge(*xt_used(layer, 1))
                    for b in range(WHI_LEAD):
                        nc.scalar.activation(ws[:, b, 0, :], h[:, b * SEQ:(b + 1) * SEQ],
                                             ACT.Copy).then_inc(*whi_done.one)

                u_turn(LAST, first_w_heads)

                def v_turn(i):
                    for j in range(RING):
                        head(i + V0 // RING, j + HI_LEAD)
                        w_head(i, j + WHI_LEAD)

                with act.Fori(0, G_TURN - 1) as i:
                    v_turn(i)
                for j in range(RING):
                    head(G_TURN - 1 + V0 // RING, j + HI_LEAD)
                    if j + WHI_LEAD == RING:
                        act.wait_ge(*w_done(layer, NK))
                    w_head(G_TURN - 1, j + WHI_LEAD)
                act.wait_ge(*x1_kept(layer, TT))
                for t in range(TT):
                    act.dma_start(x[:, t, :], x1_dram[t * P:(t + 1) * P, :]).then_inc(*x1_back.one)
                act.wait_ge(*wlo_done(layer, SEG))
                act.dma_start(ln2_g[:, :], ln_p[ds(layer * 4 + 2, 1), :].to_broadcast([P, D]))\
                   .then_inc(*ln2_in.one)
                act.dma_start(ln2_b[:, :], ln_p[ds(layer * 4 + 3, 1), :].to_broadcast([P, D]))\
                   .then_inc(*ln2_in.one)
                with act.Fori(G_TURN, LAST) as i:
                    v_turn(i)
                for j in range(RING):
                    if j + HI_LEAD < RING:
                        head(LAST + V0 // RING, j + HI_LEAD)
                    if j + WHI_LEAD < RING:
                        w_head(LAST, j + WHI_LEAD)
                nc.scalar.preload_act_table(ACT.Sqrt)
                root(1, 0)
                root(1, 1)

        @block.vector
        def _(dve):
            vec = nc.vector
            dve.wait_ge(*consts_made(0, 1))
            for t in range(TT):
                dve.wait_ge(*x_loaded[t](0, 1))
                dve.sem_inc(*x_ready.one)
                dve.sem_inc(*x_ready.one)
            with dve.Fori(0, DEPTH) as layer:
                step = Steps(dve, dve_steps, layer * DVE_STEPS, DVE_STEPS)

                def rest(turn, j):
                    turn, j = turn + j // RING, j % RING
                    dve.wait_ge(*hi_done(layer, RING * turn + (j + 1)))
                    vec.tensor_tensor(lo[:, j, :], raw[:, j, :], hi[:, j, :].bitcast(f32),
                                      ALU.subtract).then_inc(*lo_done[j].one)

                def x_rests(done):
                    for c in range(4):
                        dve.wait_ge(*xt_hi(layer, done + c + 1))
                        vec.tensor_tensor(xt[:, 2 * c:2 * c + 2, 1, :],
                                          ring_banks[c][:, :].rearrange("p (k t) -> p k t", k=2),
                                          xt[:, 2 * c:2 * c + 2, 0, :].bitcast(f32),
                                          ALU.subtract).then_inc(*xt_lo.one)

                def layer_norm(which, gain, shift, last):
                    for t in range(TT):
                        halves = [slice(c * HALF, (c + 1) * HALF) for c in range(2)]
                        if t < TT - 1:
                            dve.wait_ge(*first_summed(layer, which + 1))
                        else:
                            dve.wait_ge(*tile_used(layer, (WQ0, TILES)[which]))
                        summed = [step(vec.scalar_tensor_tensor(
                            res[:, t, cols], x[:, t, cols], ALPHA, acc_banks[2 * t + c][:, :],
                            ALU.mult, ALU.add)) for c, cols in enumerate(halves)]
                        for c, cols in enumerate(halves):
                            step.settle(summed[c])
                            step(vec.bn_stats(ln_stats[:, 12 * t + 6 * c:12 * t + 6 * c + 6],
                                              res[:, t, cols]))
                        step.settle_alone(dve_held)
                        step(vec.bn_aggr(ln_mv[:, 2 * t:2 * t + 2],
                                         ln_stats[:, 12 * t:12 * t + 12]))
                        step.settle()
                        var = ln_mv[:, 2 * t + 1:2 * t + 2]
                        vec.tensor_scalar_add(var, var, EPS).then_inc(*ln_var.one)
                        for cols in halves:
                            step(vec.scalar_tensor_tensor(
                                res[:, t, cols], res[:, t, cols], ln_mv[:, 2 * t:2 * t + 1],
                                gain[:, cols], ALU.subtract, ALU.mult))
                        dve.wait_ge(*ln_root(layer, TT * which + t + 1))
                        step(vec.reciprocal(ln_rstd[:, t:t + 1], ln_std[:, t:t + 1]))
                        step.settle()
                        for c, cols in enumerate(halves):
                            vec.scalar_tensor_tensor(
                                x[:, t, cols], res[:, t, cols], ln_rstd[:, t:t + 1],
                                shift[:, cols], ALU.mult, ALU.add).then_inc(*last.one)

                step(vec.memset(u_pad[:, :, 0:TAPS - 1], 0.0))
                x_rests(0)

                tap, tap_step = [0], [0]

                def taps(count):
                    for n in range(tap[0], tap[0] + count):
                        window, weight = u_pad[:, 0, n:n + SEQ], conv_sb[:, 0, n:n + 1]
                        if n == 0:
                            tap_step[0] = step(vec.tensor_scalar(
                                acc[:, 0, :], window, weight, conv_sb[:, 0, TAPS:TAPS + 1],
                                ALU.mult, ALU.add))
                        else:
                            step.settle(tap_step[0])
                            tap_step[0] = step(vec.scalar_tensor_tensor(
                                acc[:, 0, :], window, weight, acc[:, 0, :], ALU.mult, ALU.add))
                    tap[0] += count

                def rotate(banks, dst, before):
                    for t in range(TT):
                        if before + t:
                            dve.wait_ge(*rotated(layer, before + t))
                        src = banks[t][:, :].rearrange("p (h a d) -> p h a d", a=2, d=DH // 2)
                        cos = rope_sb[:, t, 0, :][:, None, :].to_broadcast([P, HEADS, DH])
                        sin = rope_sb[:, t, 1, :].rearrange("p (a d) -> p a d", a=2)
                        m2v = m2[:, :].rearrange("p (h a d) -> p h a d", a=2, d=DH // 2)
                        step(vec.tensor_tensor(m1[:, :].rearrange("p (h d) -> p h d", d=DH),
                                               banks[t][:, :].rearrange("p (h d) -> p h d", d=DH),
                                               cos, ALU.mult))
                        for a in range(2):
                            step(vec.tensor_tensor(
                                m2v[:, :, a, :], src[:, :, 1 - a, :],
                                sin[:, a, :][:, None, :].to_broadcast([P, HEADS, DH // 2]),
                                ALU.mult))
                        step.settle()
                        vec.tensor_tensor(dst[:, t, :], m1[:, :], m2[:, :], ALU.add)\
                           .then_inc(*rotated.one)

                for m, count in enumerate(DVE_TAPS[0]):
                    if count and not tap[0]:
                        dve.wait_ge(*params_in(layer, 5))
                    taps(count)
                    rest(0, AG0 + m + LO_LEAD)
                    c = m // 2
                    if m % 2:
                        dve.wait_ge(*sig_done(layer, c + 1))
                        step(vec.tensor_tensor(u_pad[:, c, TAPS - 1:TAPS - 1 + SEQ],
                                               ag_banks[c][0][:, 0:SEQ], sg[:, c, :], ALU.mult))
                        step.settle()
                        dve.sem_inc(*conv_u.one)
                for m, count in enumerate(DVE_TAPS[1]):
                    taps(min(count, 1))
                    rest(0, QKV0 + m + LO_LEAD)
                    if m == 5:
                        dve.wait_ge(*tile_used(layer, QKV0 + 4))
                        rotate(bank[0:2], q_sb, 0)
                    if m == 9:
                        dve.wait_ge(*tile_used(layer, QKV0 + 8))
                        rotate(bank[2:4], k_sb, TT)
                    taps(max(count - 1, 0))

                def mask_and_max(g):
                    dve.wait_ge(*sc_ps(layer, g + 1))
                    vec.tensor_tensor(sm[:, g % PROBS_RING, :], score_banks[g % 2][:, 0:3 * P],
                                      causal_sb[:, :], ALU.add).then_inc(*sc_used.one)
                    dve.wait_ge(*sc_used(layer, g + 1))
                    for t, (c0, c1) in enumerate(((0, P), (P, 3 * P))):
                        step(vec.reduce_max(row_max[:, 2 * g + t:2 * g + t + 1],
                                            sm[:, g % PROBS_RING, c0:c1], X))
                    step.settle()
                    vec.tensor_scalar(neg_max[:, 2 * g:2 * g + 2], row_max[:, 2 * g:2 * g + 2],
                                      -SCALE, None, ALU.mult).then_inc(*max_done.one)

                def normalise(g):
                    dve.wait_ge(*exp_done(layer, 2 * g + 2))
                    step(vec.reciprocal(row_inv[:, 2 * g:2 * g + 2], row_sum[:, 2 * g:2 * g + 2]))
                    step.settle()
                    here = pr[:, g % PROBS_RING]
                    step(vec.tensor_scalar(here[:, 0:P], here[:, 0:P],
                                           row_inv[:, 2 * g:2 * g + 1], None, ALU.mult))
                    vec.tensor_scalar(here[:, P:3 * P], here[:, P:3 * P],
                                      row_inv[:, 2 * g + 1:2 * g + 2], None, ALU.mult)\
                       .then_inc(*pr_done.one)

                def pv_rests(pair):
                    dve.wait_ge(*mix_hi(layer, pair + 1))
                    vec.tensor_tensor(mixed[:, pair, 1, :], pv_bank[:, 0:SEQ],
                                      mixed[:, pair, 0, :].bitcast(f32), ALU.subtract)\
                       .then_inc(*mix_lo.one)

                late, late_step = [POOL_TAPS], [0, 0]

                def late_taps(count):
                    for n in range(late[0], late[0] + count):
                        for c in range(2):
                            if n == POOL_TAPS:
                                dve.wait_ge(*prod_used(layer, POOL_TAPS - 1))
                            else:
                                step.settle(late_step[c])
                            late_step[c] = step(vec.scalar_tensor_tensor(
                                acc[:, 1 + c, :], u_pad[:, 1 + c, n:n + SEQ],
                                conv_sb[:, 1 + c, n:n + 1], acc[:, 1 + c, :], ALU.mult, ALU.add))
                    late[0] += count

                taps(DVE_TAPS[2][0])
                mask_and_max(0)
                mask_and_max(1)
                for g, count in enumerate(DVE_TAPS[3]):
                    normalise(g)
                    taps(count)
                    if g + 2 < HEADS:
                        mask_and_max(g + 2)
                    late_taps(LATE_PLAN[g])
                    if g >= 3 and g % 2:
                        pv_rests(g // 2 - 1)
                    if g == HEADS - 2:
                        step.settle()
                        dve.sem_inc(*acc_done.one)
                dve.wait_ge(*mean_ps(layer, 1))
                vec.tensor_tensor(xc[:, :, :], acc[:, :, :],
                                  mean_bank[:, None, 0:SEQ].to_broadcast([P, CT, SEQ]),
                                  ALU.subtract).then_inc(*centred.one)
                pv_rests(PAIRS - 1)
                dve.wait_ge(*var_ps(layer, 1))
                vec.tensor_scalar(rstd[:, 1, :], var_bank[:, 0:SEQ], EPS, None, ALU.add)\
                   .then_inc(*var_done.one)
                dve.wait_ge(*std_done(layer, 1))
                step(vec.reciprocal(rstd[:, 1, :], rstd[:, 0, :]))
                step.settle()
                for c in range(CT):
                    vec.tensor_tensor(xc[:, c, :], xc[:, c, :], rstd[:, 1, :], ALU.mult)\
                       .then_inc(*normed.one)
                for c in range(CT):
                    dve.wait_ge(*mix_conv_hi(layer, c + 1))
                    vec.tensor_tensor(mixed[:, PAIRS + c, 1, :], sq[:, c, :],
                                      mixed[:, PAIRS + c, 0, :].bitcast(f32), ALU.subtract)\
                       .then_inc(*mix_conv.one)

                layer_norm(0, ln1_g, ln1_b, x1_ready)
                x_rests(4)
                for n in range(WQ0, U0):
                    rest(0, n + LO_LEAD)

                def u_rests(i, mine=range(RING)):
                    for j in mine:
                        rest(i + U0 // RING, j + LO_LEAD)

                def top16(values, index, src, spare, m, now):
                    for r in range(2):
                        this = src if r == 0 else spare
                        low = slice(8 * r, 8 * r + 8)
                        for g in range(m):
                            now(vec.max(values[:, g, low], this[:, g, :]))
                        now.settle_alone(dve_held)
                        for g in range(m):
                            if r == 0:
                                now(vec.match_replace(spare[:, g, :], values[:, g, low],
                                                      this[:, g, :], LOWEST))
                            now(vec.max_index(index[:, g, low], values[:, g, low], this[:, g, :]))
                        now.settle_alone(dve_held)
                        if r == 0 and m == TOP_GROUPS:
                            dve.sem_inc(*top_in_used.one)

                A_STEPS = 5 * TOP_GROUPS + 2
                now_size = TOP_GROUPS * TOPK
                with dve.Fori(0, A_TURNS) as i:
                    now = step.turn(i, A_STEPS)
                    u_rests(i, (0,))
                    dve.wait_ge(*top_in(layer, i + 1))
                    dve.sem_inc(dve_held, 1)
                    top16(top_v8, top_i8, sg_in, sg_rest, TOP_GROUPS, now)
                    for dst, src in ((top_v, top_v8), (top_i, top_i8)):
                        now(vec.tensor_copy(
                            dst[:, :, :, :].rearrange("p t g k -> p (t g k)")[
                                :, ds(i * now_size, now_size)],
                            src[:, :, :].rearrange("p g k -> p (g k)")))
                    now.settle_alone(dve_held)
                step.ended(now, A_TURNS)

                n_sums = PAIR_HEADS * TT
                B_STEPS = 5 * n_sums + 4 * PAIR_HEADS
                top_v_flat = top_v[:, :, :, :].rearrange("p t g k -> p t (g k)")
                best_v_flat = best_v[:, :, :, :].rearrange("p t g k -> p t (g k)")
                best_c_flat = best_c[:, :, :, :].rearrange("p t g k -> p t (g k)")
                with dve.Fori(0, B_TURNS) as i:
                    now = step.turn(i, B_STEPS)
                    u_rests(i + A_TURNS, (0,))
                    for e in range(PAIR_HEADS):
                        at = i * (2 * TOPK * PAIR_HEADS) + 2 * TOPK * e
                        sums = comb[:, TT * e:TT * e + TT, :]
                        for cols, a0, n_a, n_b in ((slice(0, WIDE_SUMS), 0, WIDE, TOPK),
                                                   (slice(WIDE_SUMS, SUMS), WIDE, TOPK - WIDE,
                                                    NARROW)):
                            first = top_v_flat[:, :, ds(at + a0, n_a)]
                            second = top_v_flat[:, :, ds(at + TOPK, n_b)]
                            shape = [P, TT, n_a, n_b]
                            now(vec.tensor_tensor(
                                sums[:, :, cols].rearrange("p t (a b) -> p t a b", b=n_b),
                                first[:, :, :, None].to_broadcast(shape),
                                second[:, :, None, :].to_broadcast(shape), ALU.add))
                    now.settle_alone(dve_held)
                    top16(best_v4, best_c4, comb, comb_rest, n_sums, now)
                    for e in range(PAIR_HEADS):
                        at = ds(i * (TOPK * PAIR_HEADS) + TOPK * e, TOPK)
                        now(vec.tensor_copy(best_v_flat[:, :, at],
                                            best_v4[:, TT * e:TT * e + TT, :]))
                        now(vec.tensor_copy(best_c_flat[:, :, at],
                                            best_c4[:, TT * e:TT * e + TT, :]))
                    now.settle_alone(dve_held)
                step.ended(now, B_TURNS)
                vec.tensor_tensor(gate[:, :, :, :].rearrange("p t g k -> p (t g) k"),
                                  best_v[:, :, :, :].rearrange("p t g k -> p (t g) k"),
                                  best_v[:, :, :, 0:1].rearrange("p t g k -> p (t g) k")
                                  .to_broadcast([P, TT * PH, TOPK]),
                                  ALU.subtract).then_inc(*best_done.one)
                u_rests(A_TURNS + B_TURNS, (0,))

                def whole(t):
                    return t[:, :, :, :]

                shift, mask = ALU.logical_shift_right, ALU.bitwise_and
                step(vec.tensor_scalar(whole(row_u), whole(best_c), 4, None, shift))
                step(vec.tensor_scalar(whole(col_u), whole(best_c), 15, None, mask))
                step(vec.tensor_scalar(whole(narrow_u), whole(best_c), 2, None, shift))
                step(vec.tensor_copy(whole(place_f), whole(best_c)))
                step.settle()
                step(vec.tensor_copy(whole(row_f), whole(row_u)))
                step(vec.tensor_copy(whole(col_f), whole(col_u)))
                step(vec.tensor_copy(whole(narrow_f), whole(narrow_u)))
                step(vec.tensor_scalar(whole(is_narrow), whole(place_f), float(WIDE_SUMS), None,
                                       ALU.is_ge))
                step.settle()
                step(vec.tensor_scalar(whole(place_f), whole(narrow_f),
                                       float(WIDE - WIDE_SUMS // NARROW), None, ALU.add))
                step(vec.tensor_scalar(whole(narrow_u), whole(best_c), NARROW - 1, None, mask))
                step.settle()
                step(vec.tensor_copy(whole(narrow_f), whole(narrow_u)))
                step(vec.tensor_tensor(whole(place_f), whole(place_f), whole(row_f), ALU.subtract))
                step.settle()
                step(vec.tensor_tensor(whole(narrow_f), whole(narrow_f), whole(col_f),
                                       ALU.subtract))
                step(vec.tensor_tensor(whole(place_f), whole(place_f), whole(is_narrow), ALU.mult))
                step.settle()
                step(vec.tensor_tensor(whole(narrow_f), whole(narrow_f), whole(is_narrow),
                                       ALU.mult))
                step(vec.tensor_tensor(whole(row_f), whole(row_f), whole(place_f), ALU.add))
                step.settle()
                step(vec.tensor_tensor(whole(col_f), whole(col_f), whole(narrow_f), ALU.add))
                step.settle_alone(dve_held)

                C_STEPS = 6 * PAIR_HEADS
                top_i_flat = top_i[:, :, :, :].rearrange("p t g k -> p t (g k)")
                number = iota[:, 0:TOPK][:, None, None, :].to_broadcast([P, TT, TOPK, TOPK])
                with dve.Fori(0, C_TURNS) as i:
                    now = step.turn(i, C_STEPS)
                    for e in range(PAIR_HEADS):
                        at = ds(i * (TOPK * PAIR_HEADS) + TOPK * e, TOPK)
                        if e:
                            now.settle()
                        for half, place in enumerate((row_f, col_f)):
                            here = place[:, :, :, :].rearrange("p t g k -> p t (g k)")[:, :, at]
                            now(vec.tensor_tensor(
                                cmp[:, half], here[:, :, :, None].to_broadcast(
                                    [P, TT, TOPK, TOPK]), number, ALU.is_equal))
                        for half in range(2):
                            keys = top_i_flat[:, :, ds(i * (2 * TOPK * PAIR_HEADS)
                                                       + (2 * e + half) * TOPK, TOPK)]
                            now.settle(now.n - 1)
                            now(vec.tensor_tensor(
                                hit[:, half], cmp[:, half],
                                keys[:, :, None, :].to_broadcast([P, TT, TOPK, TOPK]), ALU.mult))
                        for half, dst in enumerate((e1, e2)):
                            now.settle(now.n - 1)
                            now(vec.tensor_reduce(
                                dst[:, :, :, :].rearrange("p t g k -> p t (g k)")[:, :, at],
                                hit[:, half], X, ALU.add))
                    u_rests(i + A_TURNS + B_TURNS + 1, (0,))
                    now.settle_alone(dve_held)
                step.ended(now, C_TURNS)
                dve.wait_ge(*gate_exp(layer, 1))
                step(vec.tensor_reduce(gate_sum[:, :, :].rearrange("p t g -> p (t g)"),
                                       gate[:, :, :, :].rearrange("p t g k -> p (t g) k"), X,
                                       ALU.add))
                step.settle()
                step(vec.reciprocal(gate_inv[:, :, :], gate_sum[:, :, :]))
                step.settle()
                vec.tensor_tensor(gate[:, :, :, :].rearrange("p t g k -> p (t g) k"),
                                  gate[:, :, :, :].rearrange("p t g k -> p (t g) k"),
                                  gate_inv[:, :, :].rearrange("p t g -> p (t g)")[:, :, None]
                                  .to_broadcast([P, TT * PH, TOPK]), ALU.mult)\
                   .then_inc(*chosen.one)
                u_rests(TOP_TURNS, (1, 2, 3))
                for t in range(TT):
                    tok = slice(t * P, (t + 1) * P)
                    dve.wait_ge(*chosen_ps(layer, t + 1))
                    step(vec.tensor_copy(i1_t[:, tok], bank[t][:, 0:P]))
                    step(vec.tensor_copy(i2_t[:, tok], bank[t][:, P:2 * P]))
                    left = bank[t][:, 2 * P:3 * P]
                    for part in range(PARTS - 1):
                        step(vec.tensor_copy(gate_part[:, part, tok], left))
                        step.settle()
                        step(vec.tensor_tensor(gate_rest[:, part, :], left,
                                               gate_part[:, part, tok], ALU.subtract))
                        step.settle()
                        left = gate_rest[:, part, :]
                    vec.tensor_copy(gate_part[:, PARTS - 1, tok], left).then_inc(*tables.one)
                    if t + 1 < TT:
                        dve.wait_ge(*tables(layer, t + 1))
                dve.wait_ge(*tables(layer, TT))
                dve.sem_inc(dve_held, 1)
                with dve.Fori(TOP_TURNS + 1, G_TURN) as i:
                    u_rests(i)

                def one_hots(seg, i, j):
                    i, j = i + j // RING, j % RING
                    tok, b = ds(i * (RING * GROUP) + j * GROUP, GROUP), j % 2
                    for dst, src, k0, n in ((one_a, i1_t, seg * SEG, SEG), (one_b, i2_t, 0, NK)):
                        last = vec.tensor_tensor(
                            dst[:, b], iota[:, k0:k0 + n][:, None, :].to_broadcast([P, GROUP, n]),
                            src[:, tok][:, :, None].to_broadcast([P, GROUP, n]), ALU.is_equal)
                    last.then_inc(*one_done.one)

                def gate_block(seg, i, j):
                    dve.wait_ge(*g_ps(layer, seg * GROUPS + RING * i + (j + 1)))
                    here = h_tok[:, ds(i * (RING * GROUP) + j * GROUP, GROUP),
                                 seg * SEG:(seg + 1) * SEG]
                    src = (acc_banks, ring_banks)[seg][j % 2][:, 0:GROUP * SEG]
                    vec.tensor_tensor(here, src.rearrange("p (t b) -> p t b", b=SEG), here,
                                      ALU.mult).then_inc(*w_done.one)

                dve.wait_ge(*x1_kept(layer, TT))
                one_hots(0, 0, 0)
                dve.wait_ge(*gelu_done(layer, SEG))
                dve.sem_inc(dve_held, 1)
                with dve.Fori(0, TURNS - G_TURN - 1) as i:
                    for j in range(RING):
                        one_hots(0, i, j + 1)
                        gate_block(0, i, j)
                        rest(i + G_TURN + U0 // RING, j + LO_LEAD)
                for j in range(RING):
                    if j + 1 < RING:
                        one_hots(0, TURNS - G_TURN - 1, j + 1)
                    else:
                        one_hots(1, 0, 0)
                    gate_block(0, TURNS - G_TURN - 1, j)
                    rest(LAST + U0 // RING, j + LO_LEAD)

                dve.wait_ge(*gelu_done(layer, NK))
                dve.sem_inc(dve_held, 1)
                with dve.Fori(0, G_TURN - 1) as i:
                    for j in range(RING):
                        one_hots(1, i, j + 1)
                        gate_block(1, i, j)
                        rest(i + V0 // RING, j + LO_LEAD)
                for j in range(RING):
                    if j + 1 < RING:
                        one_hots(1, G_TURN - 1, j + 1)
                    gate_block(1, G_TURN - 1, j)
                    rest(G_TURN - 1 + V0 // RING, j + LO_LEAD)
                with dve.Fori(G_TURN, LAST) as i:
                    for j in range(RING):
                        rest(i + V0 // RING, j + LO_LEAD)
                for j in range(RING - LO_LEAD):
                    rest(LAST + V0 // RING, j + LO_LEAD)
                dve.wait_ge(*x1_back(layer, TT))
                dve.wait_ge(*ln2_in(layer, 2))
                layer_norm(1, ln2_g, ln2_b, x_ready)
                assert step.n == DVE_STEPS, step.n

        @block.tensor
        def _(pe):
            mm = nc.tensor.matmul
            for _ in range(RING):
                pe.sem_inc(tile_used.sem, 1)
            pe.wait_ge(*consts_made(0, 1))
            with pe.Fori(0, DEPTH) as layer:

                def transpose_x(ready, before):
                    for t in range(TT):
                        for c in range(4):
                            if c % 2 == 0:
                                pe.wait_ge(*ready(layer, 2 * t + c // 2 + 1 - before))
                            for k in range(2):
                                last = nc.tensor.transpose(
                                    ring_banks[c][:, k * SEQ + t * P:k * SEQ + (t + 1) * P],
                                    x[:, t, (2 * c + k) * P:(2 * c + k + 1) * P], ident[:, :])
                            if t == TT - 1:
                                last.then_inc(*xt_ps.one)

                def tile_by_x(slot, dst, last_of_x=False, xt_before=None):
                    for k in range(KC):
                        if xt_before is not None and k % 2 == 0:
                            pe.wait_ge(*xt_lo(layer, xt_before + k // 2 + 1))
                        w_hi, w_lo = hi[:, slot, k * P:(k + 1) * P], lo[:, slot, k * P:(k + 1) * P]
                        mm(dst, w_hi, xt[:, k, 0, :], start=k == 0, stop=False)
                        mm(dst, w_hi, xt[:, k, 1, :], start=False, stop=False)
                        last = mm(dst, w_lo, xt[:, k, 0, :], start=False, stop=k == KC - 1)
                        if last_of_x and k == WHI_LEAD - 1:
                            last.then_inc(*xt_used.one)
                    last.then_inc(*tile_used.one)

                def tokens_by_tile(t, slot, stationary, chunks, banks, first, final):
                    for n, (k, col, c) in enumerate(chunks):
                        dst, cols = banks[c][:, :], slice(col, col + HALF)
                        begin = first and n < len(banks)
                        end = final and n >= len(chunks) - len(banks)
                        mm(dst, stationary(0, t, k), hi[:, slot, cols], start=begin, stop=False)
                        mm(dst, stationary(0, t, k), lo[:, slot, cols], start=False, stop=False)
                        last = mm(dst, stationary(1, t, k), hi[:, slot, cols], start=False,
                                  stop=end)
                    return last

                def by_tile(slot, stationary, chunks, banks, first, final):
                    for t in range(TT):
                        last = tokens_by_tile(t, slot, stationary, chunks, banks[t], first, final)
                    last.then_inc(*tile_used.one)

                def last_tiles(wait, stationary):
                    for t in range(TT):
                        for j in range(RING):
                            if t == 0:
                                wait(j)
                            last = tokens_by_tile(
                                t, j, lambda part, t, k, j=j: stationary(part, t, j),
                                [(0, 0, 0), (0, HALF, 1)], model_banks[t], False,
                                j == RING - 1)
                            if t == TT - 1:
                                last.then_inc(*tile_used.one)
                        if t == 0:
                            last.then_inc(*first_summed.one)

                def x_part(part, t, k):
                    return xt[:, k, part, t * P:(t + 1) * P]

                def mixed_part(part, t, k):
                    return mixed[:, k, part, t * P:(t + 1) * P]

                model_banks = [[acc_banks[2 * t], acc_banks[2 * t + 1]] for t in range(TT)]

                transpose_x(x_ready, 2 * TT)
                def qk_transposed(c):
                    src, b = ((q_sb, 6), (q_sb, 7), (k_sb, 0), (k_sb, 1))[c]
                    pe.wait_ge(*rotated(layer, 2 if c < 2 else 4))
                    for k in range(2):
                        pair = 2 * (c % 2) + k
                        for t in range(TT):
                            last = nc.tensor.transpose(
                                bank[b][:, k * SEQ + t * P:k * SEQ + (t + 1) * P],
                                src[:, t, pair * P:(pair + 1) * P], ident[:, :])
                    last.then_inc(*qk_ps.one)

                def conv_pair(c):
                    for e in range(2):
                        n = AG0 + 2 * c + e
                        pe.wait_ge(*lo_done[n % RING](layer, n // RING + 1))
                        tile_by_x(n % RING, ag_banks[c][e][:, 0:SEQ],
                                  xt_before=0 if n == AG0 else None)

                for c in range(CT):
                    conv_pair(c)

                for g in range(3):
                    pe.wait_ge(*conv_u(layer, g + 1))
                    for m in range(4):
                        n = QKV0 + 4 * g + m
                        pe.wait_ge(*lo_done[n % RING](layer, n // RING + 1))
                        by_tile(n % RING, x_part, [(2 * m, 0, 0), (2 * m + 1, HALF, 0)],
                                [[bank[2 * g]], [bank[2 * g + 1]]], m == 0, m == 3)
                        if n == WO0 - 3:
                            pe.wait_ge(*conv_u(layer, CT))
                            qk_transposed(0)
                            qk_transposed(1)
                qk_transposed(2)
                qk_transposed(3)

                taps_done = [0]

                def conv_taps(count):
                    for tap in range(taps_done[0], taps_done[0] + count):
                        last = mm(conv_bank[:, 0:SEQ], diag[:, tap, :], u_pad[:, 3, tap:tap + SEQ],
                                  start=tap == 0, stop=tap == TAPS - 1)
                        if tap == TAPS - 1:
                            last.then_inc(*conv_ps.one)
                    taps_done[0] += count

                def scores(g):
                    if g >= 2:
                        pe.wait_ge(*sc_used(layer, g - 1))
                    rows = slice(DH * (g % 2), DH * (g % 2) + DH)
                    mm(score_banks[g % 2][:, 0:P], q_t[rows, g // 2, 0:P], k_t[rows, g // 2, 0:P],
                       start=True, stop=True)
                    mm(score_banks[g % 2][:, P:3 * P], q_t[rows, g // 2, P:2 * P],
                       k_t[rows, g // 2, :], start=True, stop=True).then_inc(*sc_ps.one)

                def probs_transposed(g):
                    pe.wait_ge(*pr_done(layer, g + 1))
                    if g >= 1:
                        pe.wait_ge(*pt_done(layer, g))
                    for c in range(3):
                        last = nc.tensor.transpose(pt_bank[:, c * P:(c + 1) * P],
                                                   pr[:, g % PROBS_RING, c * P:(c + 1) * P],
                                                   ident[:, :])
                    last.then_inc(*pt_ps.one)

                def weighted_values(pair):
                    if pair:
                        pe.wait_ge(*mix_lo(layer, pair))
                    for e in range(2):
                        g = 2 * pair + e
                        pe.wait_ge(*pt_done(layer, g + 1))
                        rows, cols = slice(DH * e, DH * e + DH), slice(g * DH, (g + 1) * DH)
                        mm(pv_bank[rows, 0:SEQ], v_sb[:, 0, cols],
                           p_t[:, g % PROBS_RING, 0:2 * P], start=True, stop=False)
                        last = mm(pv_bank[rows, P:SEQ], v_sb[:, 1, cols],
                                  p_t[:, g % PROBS_RING, 2 * P:3 * P], start=False, stop=True)
                    last.then_inc(*pv_ps.one)

                pe.wait_ge(*qk_done(layer, 4))
                scores(0)
                scores(1)
                pe.wait_ge(*diags_made(layer, 1))
                conv_taps(PE_TAPS[2][0])
                pe.wait_ge(*v_done(layer, TT))

                def project(m):
                    n = WO0 + m
                    pe.wait_ge(*lo_done[n % RING](layer, n // RING + 1))
                    by_tile(n % RING, mixed_part, [(m, 0, 0), (m, HALF, 1)], model_banks,
                            m == 0, m == KC - 1)

                for g, count in enumerate(PE_TAPS[3]):
                    if g + 2 < HEADS:
                        scores(g + 2)
                    conv_taps(count)
                    if g == HEADS - 1:
                        pe.wait_ge(*sc_used(layer, HEADS))
                        pe.wait_ge(*acc_done(layer, 1))
                        for c in range(CT):
                            last = mm(mean_bank[:, 0:SEQ], ones[:, :], acc[:, c, :], start=c == 0,
                                      stop=c == CT - 1)
                        last.then_inc(*mean_ps.one)
                    probs_transposed(g)
                    if g >= 2 and g % 2 == 0:
                        weighted_values(g // 2 - 1)
                    if g == HEADS - 2:
                        pe.wait_ge(*conv_out(layer, 1))
                        pe.wait_ge(*mix_lo(layer, 1))
                        project(0)
                weighted_values(PAIRS - 1)
                pe.wait_ge(*mix_lo(layer, 2))
                project(1)
                pe.wait_ge(*sq_done(layer, 1))
                for c in range(CT):
                    last = mm(var_bank[:, 0:SEQ], ones[:, :], sq[:, c, :], start=c == 0,
                              stop=c == CT - 1)
                last.then_inc(*var_ps.one)
                pe.wait_ge(*mix_lo(layer, 3))
                project(2)
                pe.wait_ge(*mix_lo(layer, 4))
                project(3)


                def conv_chunk_ready(c):
                    n = WO0 + PAIRS + c
                    pe.wait_ge(*mix_conv(layer, c + 1))
                    pe.wait_ge(*lo_done[n % RING](layer, n // RING + 1))

                last_tiles(conv_chunk_ready, lambda part, t, c: mixed_part(part, t, PAIRS + c))
                transpose_x(x1_ready, 0)
                for n in range(WQ0, U0):
                    pe.wait_ge(*lo_done[n % RING](layer, n // RING + 1))
                    if n >= WQ0 + 8:
                        pe.wait_ge(*qp_done(layer, n - WQ0 - 7))
                    tile_by_x(n % RING, bank[n % 8][:, 0:SEQ], xt_before=4 if n == WQ0 else None)
                pe.wait_ge(*qp_done(layer, HC))
                pe.wait_ge(*keys_in(layer, 1))
                for t in range(TT):
                    for c in range(4):
                        for k in range(4):
                            g = 4 * c + k
                            last = mm(bank[(4 + 4 * t + c) % 8][:, k * NK:(k + 1) * NK],
                                      qp_t[:, g, t * P:(t + 1) * P], keys_sb[:, g, :],
                                      start=True, stop=True)
                        last.then_inc(*sp_ps.one)

                def u_tile(i, j, last_of_x=False):
                    pe.wait_ge(*lo_done[j](layer, i + (U0 // RING + 1)))
                    pe.wait_ge(*gelu_done(layer, RING * i + (j - RING + 1)))
                    tile_by_x(j, ring_banks[j][:, 0:SEQ], last_of_x)

                def gate_matrices(seg, i, j):
                    pe.wait_ge(*gated_done(layer, seg * GROUPS + RING * i + (j + 1)))
                    pe.wait_ge(*w_done(layer, seg * GROUPS + RING * i + (j - 1)))
                    b = j % 2
                    for t in range(GROUP):
                        dst = (acc_banks, ring_banks)[seg][b][:, t * SEG:(t + 1) * SEG]
                        for part in range(PARTS):
                            last = mm(dst, one_b[:, b, t, :], gated_a[:, b, part, t, :],
                                      start=part == 0, stop=part == PARTS - 1)
                    last.then_inc(*g_ps.one)

                pe.wait_ge(*s_done(layer, 4))
                pe.sem_inc(pe_held, 1)
                with pe.Fori(0, TOP_TURNS + 1) as i:
                    for j in range(RING):
                        u_tile(i, j)
                pe.wait_ge(*chosen(layer, 1))
                for t in range(TT):
                    for c, src in enumerate((e1, e2, gate)):
                        last = nc.tensor.transpose(
                            bank[t][:, c * P:(c + 1) * P],
                            src[:, t].rearrange("p g k -> p (g k)"), ident[:, :])
                    last.then_inc(*chosen_ps.one)
                with pe.Fori(TOP_TURNS + 1, G_TURN) as i:
                    for j in range(RING):
                        u_tile(i, j)
                with pe.Fori(0, TURNS - G_TURN - 1) as i:
                    for j in range(RING):
                        gate_matrices(0, i, j)
                        u_tile(i + G_TURN, j)
                for j in range(RING):
                    gate_matrices(0, TURNS - G_TURN - 1, j)
                    u_tile(LAST, j, j == RING - 1)

                def v_part(j):
                    return lambda part, t, k: ws[:, j, part, t * P:(t + 1) * P]

                def v_turn(i, first=False, gates=False):
                    for j in range(RING):
                        if gates:
                            gate_matrices(1, i, j)
                        v_ready(i, j)
                        by_tile(j, v_part(j), [(0, 0, 0), (0, HALF, 1)], model_banks,
                                first and j == 0, False)

                def v_ready(i, j):
                    pe.wait_ge(*lo_done[j](layer, i + (V0 // RING + 1)))
                    pe.wait_ge(*wlo_done(layer, RING * i + (j + 1)))

                pe.wait_ge(*gelu_done(layer, NK - 2))
                v_turn(0, first=True, gates=True)
                with pe.Fori(1, G_TURN) as i:
                    v_turn(i, gates=True)
                with pe.Fori(G_TURN, LAST) as i:
                    v_turn(i)
                last_tiles(lambda j: v_ready(LAST, j), lambda part, t, j: v_part(j)(part, t, 0))


def rope_table():
    inv = np.power(np.float32(10000.0), -np.arange(0, DH, 2, dtype=np.float32) / DH)
    ang = np.arange(SEQ, dtype=np.float32)[:, None] * inv[None, :].astype(np.float32)
    cos, sin = np.cos(ang), np.sin(ang)
    both = np.stack([np.concatenate([cos, cos], 1), np.concatenate([-sin, sin], 1)], 1)
    return both.reshape(TT, P, 2, DH).transpose(1, 0, 2, 3).astype(np.float32)


def causal_table():
    tri = np.where(np.arange(P)[None, :] <= np.arange(P)[:, None], 0.0, MASKED)
    return np.concatenate([tri, np.zeros((P, P)), tri], 1).astype(np.float32)


def kernel(x, w_in, conv_w, conv_b, conv_ln_g, conv_ln_b, w_out, ln1_g, ln1_b,
           peer_wq, peer_keys, peer_u, peer_v, ln2_g, ln2_b):
    import concourse.bacc as bacc
    from concourse.bass_utils import run_bass_kernel_spmd

    w_in, w_out, peer_wq, peer_u, peer_v = map(np.asarray, (w_in, w_out, peer_wq, peer_u, peer_v))
    L = DEPTH
    ag = w_in[:, :, 3 * AW:].reshape(L, KC, P, 2, CT, P).transpose(0, 4, 3, 2, 1, 5)
    qkv = w_in[:, :, :3 * AW].reshape(L, KC // 2, 2, P, 3, AW).transpose(0, 4, 1, 3, 2, 5)
    wq = peer_wq.reshape(L, KC, P, HC, P).transpose(0, 3, 2, 1, 4)
    u = peer_u.reshape(L, NK, NK, KC, P).transpose(0, 1, 4, 3, 2)
    stream = np.concatenate([ag.reshape(L, -1, D), qkv.reshape(L, -1, D), w_out,
                             wq.reshape(L, -1, D), u.reshape(L, -1, D),
                             peer_v.reshape(L, -1, D)], axis=1).reshape(-1, D)
    keys_t = np.asarray(peer_keys).transpose(0, 4, 1, 2, 3).reshape(L * P, HC * NK)
    conv_p = np.concatenate([np.asarray(conv_w), np.asarray(conv_b)[:, None],
                             np.asarray(conv_ln_g)[:, None], np.asarray(conv_ln_b)[:, None]], 1)
    conv_p = conv_p.reshape(L, TAPS + 3, CT, P).transpose(0, 3, 2, 1).reshape(L * P, -1)
    ln_p = np.stack([np.asarray(a) for a in (ln1_g, ln1_b, ln2_g, ln2_b)], 1).reshape(L * 4, D)
    arrays = {
        "x": np.asarray(x).reshape(SEQ, D), "stream": stream, "keys_t": keys_t, "conv_p": conv_p,
        "ln_p": ln_p, "rope": rope_table().reshape(P, -1), "causal": causal_table(),
    }
    arrays = {name: np.ascontiguousarray(a) for name, a in arrays.items()}

    nc = bacc.Bacc("TRN2", target_bir_lowering=False, num_devices=1)
    args = [nc.dram_tensor(f"in_{name}", a.shape, mybir.dt.float32, kind="ExternalInput").ap()
            for name, a in arrays.items()]
    result = nc.dram_tensor("result", (SEQ, D), mybir.dt.float32, kind="ExternalOutput").ap()
    x1_dram = nc.dram_tensor("x1_kept", (SEQ, D), mybir.dt.float32, kind="Internal").ap()
    build(nc, *args, x1_dram, result)
    r = run_bass_kernel_spmd(nc, [{f"in_{name}": a for name, a in arrays.items()}], core_ids=[0])
    return np.asarray(r.results[0]["result"]).reshape(1, SEQ, D)
```
